# Optimizing a Trainium2 kernel written in Bass

```python
import jax, jax.numpy as jnp
from jax import lax
import numpy as np

D_MODEL = 1024
BATCH = 1
SEQ = 512
DEPTH = 1

CHUNK = 64
N_HEADS = 8
HEAD_DIM = 64
D_ATTN = N_HEADS * HEAD_DIM
LEFT_CHUNKS = 8
BAND = (LEFT_CHUNKS + 1) * CHUNK
REL_CLIP = 128
N_REL = 2 * REL_CLIP + 1
D_CONV = D_MODEL // 2
CONV_W = 31
N_BRANCH = 2
D_IN = 2 * D_CONV + 3 * D_ATTN + N_BRANCH * D_MODEL
PEER_HEADS = 8
PEER_NKEYS = 128
PEER_N = PEER_NKEYS * PEER_NKEYS
PEER_DQ = 256
PEER_DH = PEER_DQ // 2
PEER_TOPK = 16
PEER_BLOCK = 128
EPS = 1e-6
NEG_INF = -1e30

kernel_name = 'hybrid_conv_chunkattn_peer_adaln'

def rms_norm(x, g):
    xf = x.astype(jnp.float32)
    y = xf * lax.rsqrt(jnp.mean(xf * xf, axis=-1, keepdims=True) + EPS)
    return (y * g.astype(jnp.float32)).astype(x.dtype)

def layer_norm(x, g, b):
    xf = x.astype(jnp.float32)
    mu = jnp.mean(xf, axis=-1, keepdims=True)
    var = jnp.mean(jnp.square(xf - mu), axis=-1, keepdims=True)
    y = (xf - mu) * lax.rsqrt(var + EPS)
    return (y * g.astype(jnp.float32) + b.astype(jnp.float32)).astype(x.dtype)

def conv_module(a, b, conv_dw, conv_b, ln_g, ln_b, w_conv_out):
    u = a * jax.nn.sigmoid(b)
    y = lax.conv_general_dilated(
        u, conv_dw[:, None, :].astype(u.dtype), window_strides=(1,),
        padding=[(CONV_W - 1, 0)], dimension_numbers=('NWC', 'WIO', 'NWC'),
        feature_group_count=D_CONV) + conv_b
    y = jax.nn.silu(layer_norm(y, ln_g, ln_b))
    return y @ w_conv_out

def chunked_attention(q, k, v, q_norm_g, k_norm_g, rel_bias, w_attn_out):
    B, S, _ = q.shape
    nc = S // CHUNK
    q = rms_norm(q.reshape(B, S, N_HEADS, HEAD_DIM), q_norm_g)
    k = rms_norm(k.reshape(B, S, N_HEADS, HEAD_DIM), k_norm_g)
    v = v.reshape(B, S, N_HEADS, HEAD_DIM)
    qc = q.reshape(B, nc, CHUNK, N_HEADS, HEAD_DIM)
    pad = ((0, 0), (LEFT_CHUNKS * CHUNK, 0), (0, 0), (0, 0))
    kp = jnp.pad(k, pad).reshape(B, nc + LEFT_CHUNKS, CHUNK, N_HEADS, HEAD_DIM)
    vp = jnp.pad(v, pad).reshape(B, nc + LEFT_CHUNKS, CHUNK, N_HEADS, HEAD_DIM)
    band_idx = jnp.arange(nc)[:, None] + jnp.arange(LEFT_CHUNKS + 1)[None, :]
    kb = kp[:, band_idx].reshape(B, nc, BAND, N_HEADS, HEAD_DIM)
    vb = vp[:, band_idx].reshape(B, nc, BAND, N_HEADS, HEAD_DIM)
    s = jnp.einsum('bnqhd,bnkhd->bnhqk', qc, kb,
                   preferred_element_type=jnp.float32) * (HEAD_DIM ** -0.5)
    qpos = LEFT_CHUNKS * CHUNK + jnp.arange(CHUNK)
    kpos = jnp.arange(BAND)
    rel = jnp.clip(qpos[:, None] - kpos[None, :], -REL_CLIP, REL_CLIP) + REL_CLIP
    bias = rel_bias[:, rel].astype(jnp.float32)
    key_chunk = jnp.arange(nc)[:, None] - LEFT_CHUNKS + kpos[None, :] // CHUNK
    valid = key_chunk >= 0
    s = jnp.where(valid[None, :, None, None, :], s + bias[None, None], NEG_INF)
    p = jax.nn.softmax(s, axis=-1).astype(v.dtype)
    o = jnp.einsum('bnhqk,bnkhd->bnqhd', p, vb).reshape(B, S, D_ATTN)
    return o @ w_attn_out

def peer_ffn(h, peer_wq, peer_keys, peer_u, peer_v):
    B, S, D = h.shape
    T = B * S
    ht = h.reshape(T, D)
    q = (ht @ peer_wq).reshape(T, PEER_HEADS, 2, PEER_DH)
    s = jnp.einsum('thpd,hpkd->thpk', q, peer_keys,
                   preferred_element_type=jnp.float32)
    sv, si = lax.top_k(s, PEER_TOPK)
    cand = (sv[..., 0, :, None] + sv[..., 1, None, :]).reshape(T, PEER_HEADS, PEER_TOPK * PEER_TOPK)
    cidx = (si[..., 0, :, None] * PEER_NKEYS + si[..., 1, None, :]).reshape(T, PEER_HEADS, PEER_TOPK * PEER_TOPK)
    top, pos = lax.top_k(cand, PEER_TOPK)
    eidx = jnp.take_along_axis(cidx, pos, axis=-1)
    g = jax.nn.softmax(top, axis=-1).astype(h.dtype)
    nb = T // PEER_BLOCK

    def expert_block(args):
        hb, ib, gb = args
        u = peer_u[ib]
        a = jax.nn.gelu(jnp.einsum('td,thkd->thk', hb, u), approximate=False)
        return jnp.einsum('thk,thkd->td', gb * a, peer_v[ib])

    out = lax.map(expert_block, (ht.reshape(nb, PEER_BLOCK, D),
                                 eidx.reshape(nb, PEER_BLOCK, PEER_HEADS, PEER_TOPK),
                                 g.reshape(nb, PEER_BLOCK, PEER_HEADS, PEER_TOPK)))
    return out.reshape(B, S, D)

def setup_inputs(seed: int = 0) -> dict:
    key = jax.random.key(seed)
    ks = jax.random.split(key, 24)
    f32 = jnp.float32

    def nrm(k, shape, scale):
        return jax.random.normal(k, shape, f32) * scale

    L, D = DEPTH, D_MODEL
    return {
        'x': nrm(ks[0], (BATCH, SEQ, D), 1.0),
        'c': nrm(ks[1], (BATCH, D), 1.0),
        'w_ada': nrm(ks[2], (L, D, 6 * D), 0.5 * D ** -0.5),
        'b_ada': nrm(ks[3], (L, 6 * D), 0.02),
        'norm1_g': 1.0 + nrm(ks[4], (L, D), 0.1),
        'norm2_g': 1.0 + nrm(ks[5], (L, D), 0.1),
        'w_in': nrm(ks[6], (L, D, D_IN), D ** -0.5),
        'conv_dw': nrm(ks[7], (L, CONV_W, D_CONV), CONV_W ** -0.5),
        'conv_b': nrm(ks[8], (L, D_CONV), 0.02),
        'conv_ln_g': 1.0 + nrm(ks[9], (L, D_CONV), 0.1),
        'conv_ln_b': nrm(ks[10], (L, D_CONV), 0.02),
        'w_conv_out': nrm(ks[11], (L, D_CONV, D), D_CONV ** -0.5),
        'q_norm_g': 1.0 + nrm(ks[12], (L, HEAD_DIM), 0.1),
        'k_norm_g': 1.0 + nrm(ks[13], (L, HEAD_DIM), 0.1),
        'rel_bias': nrm(ks[14], (L, N_HEADS, N_REL), 0.5),
        'w_attn_out': nrm(ks[15], (L, D_ATTN, D), D_ATTN ** -0.5),
        'w_out': nrm(ks[16], (L, D, D), D ** -0.5),
        'peer_wq': nrm(ks[17], (L, D, PEER_HEADS * PEER_DQ), D ** -0.5),
        'peer_keys': nrm(ks[18], (L, PEER_HEADS, 2, PEER_NKEYS, PEER_DH), PEER_DH ** -0.5),
        'peer_u': nrm(ks[19], (L, PEER_N, D), D ** -0.5),
        'peer_v': nrm(ks[20], (L, PEER_N, D), PEER_HEADS ** -0.5),
    }

def reference(x, c, w_ada, b_ada, norm1_g, norm2_g, w_in, conv_dw, conv_b, conv_ln_g,
              conv_ln_b, w_conv_out, q_norm_g, k_norm_g, rel_bias, w_attn_out, w_out,
              peer_wq, peer_keys, peer_u, peer_v):
    split_pts = [D_CONV, 2 * D_CONV, 2 * D_CONV + D_ATTN,
                 2 * D_CONV + 2 * D_ATTN, 2 * D_CONV + 3 * D_ATTN, 2 * D_CONV + 3 * D_ATTN + D_MODEL]
    cond = jax.nn.silu(c)
    for l in range(DEPTH):
        mod = (cond @ w_ada[l] + b_ada[l])[:, None, :]
        sh1, sc1, ga1, sh2, sc2, ga2 = jnp.split(mod, 6, axis=-1)
        h = rms_norm(x, norm1_g[l]) * (1.0 + sc1) + sh1
        proj = h @ w_in[l]
        glu_a, glu_b, q, k, v, gl_conv, gl_attn = jnp.split(proj, split_pts, axis=-1)
        y_conv = conv_module(glu_a, glu_b, conv_dw[l], conv_b[l], conv_ln_g[l],
                             conv_ln_b[l], w_conv_out[l])
        y_attn = chunked_attention(q, k, v, q_norm_g[l], k_norm_g[l], rel_bias[l], w_attn_out[l])
        merged = jax.nn.sigmoid(gl_conv) * y_conv + jax.nn.sigmoid(gl_attn) * y_attn
        x = x + ga1 * (merged @ w_out[l])
        h2 = rms_norm(x, norm2_g[l]) * (1.0 + sc2) + sh2
        x = x + ga2 * peer_ffn(h2, peer_wq[l], peer_keys[l], peer_u[l], peer_v[l])
    return x


_drawn_inputs = setup_inputs


def setup_inputs(seed=0):
    import zlib

    import numpy as np

    out = dict(_drawn_inputs(seed))
    spreads = {}
    factors = {'b_ada': 4.096,
     'norm1_g': 4.14,
     'norm2_g': 2.697,
     'conv_b': 8.0,
     'conv_ln_g': 4.216,
     'conv_ln_b': 23.077,
     'q_norm_g': 8.0,
     'k_norm_g': 8.0,
     'rel_bias': 4.995}
    for name, (base, spread) in spreads.items():
        noise = np.random.default_rng([zlib.crc32(name.encode()), seed]).standard_normal(out[name].shape)
        drawn = base * np.exp(spread * noise) if base else spread * noise
        out[name] = __import__('jax').numpy.asarray(drawn.astype(out[name].dtype))
    for name, factor in factors.items():
        out[name] = (out[name] * factor).astype(out[name].dtype)
    return out
```

```python
from contextlib import ExitStack

import numpy as np

import concourse.bass as bass
from concourse import mybir

ACT = mybir.ActivationFunctionType
ALU = mybir.AluOpType
AX = mybir.AxisListType
F32 = mybir.dt.float32
F32R = mybir.dt.float32r
U32 = mybir.dt.uint32

P = 128
T = 512
D = 1024
DC = D // P
TT = T // P
EPS = 1e-6
HEADS = 8
HD = 64
CHUNK = 64
TAPS = 31
CC = 4
PH = 8
TOPK = 16
NKEY = 128
LOWEST = -3.0e38
MASKED = -1e30
RING = 4

COL = {}
_at = 0
for _name, _n in (("c", DC), ("b_ada", 6 * DC), ("g1", DC), ("g2", DC), ("dw", CC * TAPS), ("conv_b", CC),
                  ("ln_g", CC), ("ln_b", CC), ("qg", 1), ("kg", 1)):
    COL[_name] = (_at, _n)
    _at += _n
PAR_COLS = _at

GLU0, QK0, V0, MIX0 = 0, 8, 16, 20
MIX = []
for _m in range(DC):
    MIX += [("gate", _m, 0), ("gate", _m, 1)]
    if _m == 1:
        MIX += [("out", 0), ("out", 1)]
    if _m > 1:
        MIX += [("out", _m)]
WOUT0 = MIX0 + len(MIX)
WQ0 = WOUT0 + DC
FRONT = WQ0 + 2 * PH
SLABS = 8
GROUPS = NKEY // SLABS
TB = 32
ADA = 6 * DC
ADA_FIRST = 2 * DC


def block_program(nc, w_front, w_ada, par_d, const_d, selt_d, x_d, toep_d, keys_d, u_d, v_d, g_d, out_d):
    ctx = ExitStack()
    with ctx:
        def sb(name, shape, dt=F32):
            return ctx.enter_context(nc.sbuf_tensor("sb_" + name, shape, dt))

        def sem(name):
            return ctx.enter_context(nc.semaphore(name))

        w_hi = sb("w_hi", [P, RING, 1024], F32R)
        w_lo = sb("w_lo", [P, RING, 1024], F32R)
        act_hi = sb("act_hi", [P, DC, T], F32R)
        act_lo = sb("act_lo", [P, DC, T], F32R)
        mix_hi = sb("mix_hi", [P, DC, T], F32R)
        mix_lo = sb("mix_lo", [P, DC, T], F32R)
        stage = sb("stage", [P, RING, 1024])
        x = sb("x", [P, DC, T])
        wide = sb("wide", [P, DC, T])
        par = sb("par", [P, PAR_COLS])
        const = sb("const", [P, 5 * P])
        selt = sb("selt", [16, 8 * P])
        mod = sb("mod", [P, ADA])
        small = sb("small", [P, 160])
        scr = sb("scr", [P, 13952])

        ident = const[:, 0:P]
        ones = const[:, P:2 * P]
        iota = const[:, 2 * P:3 * P]
        sel = const[:, 3 * P:4 * P].rearrange("p (m c) -> p m c", c=16)
        iota16 = const[:, 4 * P:4 * P + 16]

        def col(name, i=0, n=1):
            return par[:, COL[name][0] + i:COL[name][0] + i + n]

        def at(off, shape):
            n = int(np.prod(shape))
            v = scr[:, off:off + n]
            if len(shape) == 2:
                return v.rearrange("p (a b) -> p a b", b=shape[1])
            if len(shape) == 3:
                return v.rearrange("p (a b c) -> p a b c", b=shape[1], c=shape[2])
            return v

        vtok = at(0, [TT, 512])
        y = at(2048, [CC, T])
        U_W = TAPS - 1 + T
        u = at(4096, [CC, U_W])
        toep = at(6272, [2, T])
        r1 = 7296
        ada = at(r1, [4, 1024])
        pt = at(r1, [2, TT, T])
        gate = at(r1, [4, T])
        sq = at(11392, [2, T])
        rstd = at(12416, [T])
        sc = at(11392, [3, T])
        tmp = at(12928, [2, T])
        scores = at(0, [TT, 2 * PH, NKEY])
        keys = at(8192, [2 * PH, NKEY])
        qf = at(10240, [2, T])
        IJW = 3
        wf = wide[:, :, :].rearrange("p a b -> p (a b)")

        def wat(off, n):
            return wf[:, off:off + n]

        sv = wat(0, 1024).rearrange("p (t c k) -> p t c k", t=TT, c=16)
        si = wat(1024, 1024).bitcast(U32).rearrange("p (t c k) -> p t c k", t=TT, c=16)
        top = wat(2048, 512).rearrange("p (t h k) -> p t h k", t=TT, h=PH)
        pos = wat(2560, 512).bitcast(U32).rearrange("p (t h k) -> p t h k", t=TT, h=PH)
        ijw = wat(3072, 3 * P).rearrange("p (c k) -> p c k", c=3)
        rank = wat(3456, 2 * P).rearrange("p (c k) -> p c k", c=2)
        ranku = wat(3712, 2 * P).bitcast(U32).rearrange("p (c k) -> p c k", c=2)
        sif = at(12928, [256])
        hot16 = scr[:, 8192:8192 + 2048]
        mr = at(12928, [2, NKEY])
        cand = at(13184, [256])
        cand2 = at(13440, [256])
        gb = at(0, [2, NKEY, TB])
        hot = scr[:, 8192:8192 + 2048].rearrange("p (s a b) -> p s a b", s=8, a=2)
        ijt = at(10240, [3, T])
        gtile = scr[:, 0:4096].rearrange("p (s b j t) -> p s b j t", s=2, b=T // TB, j=4)
        ga = at(4096, [2, T])
        cf = at(5120, [2, T])
        fin = at(6144, [2, T])

        bank = [ctx.enter_context(nc.psum_tensor(f"bank{b}", [P, 512], F32)) for b in range(8)]
        MODB, STAT, XB = bank[0], bank[1], (bank[2], bank[3])
        UB = bank[4:8]

        par_in = sem("par_in")
        x_in = sem("x_in")
        selt_in = sem("selt_in")
        ada_in = [sem(f"ada_in{i}") for i in range(4)]
        w_in = [sem(f"w_in{i}") for i in range(RING)]
        toep_in = [sem(f"toep_in{i}") for i in range(2)]
        keys_in = sem("keys_in")
        gt_in = [sem(f"gt_in{i}") for i in range(2)]
        gw_out = [sem(f"gw_out{i}") for i in range(2)]
        out_in = [sem(f"out_in{i}") for i in range(2)]
        w_round = sem("w_round")
        w_split = sem("w_split")
        w_used = sem("w_used")
        cond_ok = sem("cond_ok")
        ada_used = sem("ada_used")
        mod_ok = sem("mod_ok")
        sq_ok = sem("sq_ok")
        sq_used = sem("sq_used")
        ms_ok = sem("ms_ok")
        rt_ok = sem("rt_ok")
        a_pre = sem("a_pre")
        a_hi = sem("a_hi")
        a_lo = sem("a_lo")
        step = sem("step")
        sig_ok = sem("sig_ok")
        u_ok = sem("u_ok")
        qk_ok = sem("qk_ok")
        rb_ok = sem("rb_ok")
        qkn_ok = sem("qkn_ok")
        v_ok = sem("v_ok")
        msk_ok = sem("msk_ok")
        s_ok = sem("s_ok")
        sb_ok = sem("sb_ok")
        e_ok = sem("e_ok")
        p_ok = sem("p_ok")
        t_ok = sem("t_ok")
        pt_ok = sem("pt_ok")
        o_ok = sem("o_ok")
        conv_ok = sem("conv_ok")
        y_sum = sem("y_sum")
        y_ok = sem("y_ok")
        y_act = sem("y_act")
        y_nrm = sem("y_nrm")
        m_ok = sem("m_ok")
        x2_ok = sem("x2_ok")
        qf_ok = sem("qf_ok")
        ks_ok = sem("ks_ok")
        sc_ok = sem("sc_ok")
        tk_ok = sem("tk_ok")
        te_ok = sem("te_ok")
        ijw_ok = sem("ijw_ok")
        ijt_ok = sem("ijt_ok")
        ijt_cp = sem("ijt_cp")
        hot_ok = sem("hot_ok")
        g_ok = sem("g_ok")
        g_cp = sem("g_cp")
        ge_ok = sem("ge_ok")
        c_mul = sem("c_mul")
        c_hi = sem("c_hi")
        c_lo = sem("c_lo")
        v_part = sem("v_part")
        acc_ok = sem("acc_ok")
        fin_ok = sem("fin_ok")

        def sums_read(n):
            if n < QK0:
                return (sig_ok if n % 2 == 0 else u_ok), n // 2 + 1
            if n < V0:
                return sq_ok, DC + n - QK0 + 1
            if n < MIX0:
                return v_ok, n - V0 + 1
            if n < WOUT0:
                kind = MIX[n - MIX0]
                return (m_ok, kind[1] + 1) if kind[0] == "out" else (sig_ok, CC + 2 * kind[1] + kind[2] + 1)
            return (x2_ok, n - WOUT0 + 1) if n < WQ0 else (qf_ok, n - WQ0 + 1)

        block = ctx.enter_context(nc.Block())

        @block.sync
        def _(sp):
            sp.dma_start(x[:, :, :], x_d.rearrange("c p t -> p c t")).then_inc(x_in, 16)

            def load(n, src):
                if not isinstance(n, int) or n >= RING:
                    sp.wait_ge(w_split, n - RING + 1)
                return sp.dma_start(stage[:, slot, :], src.rearrange("a p n -> p (a n)"))

            for n in range(RING):
                slot = n
                load(n, w_front[n:n + 1]).then_inc(w_in[slot], 16)
            with sp.Fori(1, FRONT // RING) as turn:
                for slot in range(RING):
                    n = turn * RING + slot
                    load(n, w_front[bass.ds(n, 1)]).then_inc(w_in[slot], 16)
            with sp.Fori(0, GROUPS) as g:
                for half in range(4):
                    src_d = u_d if half < 2 else v_d
                    for slot in range(RING):
                        n = g * (2 * SLABS) + (FRONT + half * RING + slot)
                        k = g * SLABS + (half % 2 * RING + slot)
                        load(n, src_d[bass.ds(k, 1)]).then_inc(w_in[slot], 16)
            for m in range(DC):
                sp.wait_ge(fin_ok, m + 1)
                sp.dma_start(out_d[m], fin[:, m % 2, :]).then_inc(out_in[m % 2], 16)
            for i in range(2):
                sp.wait_ge(out_in[i], 16 * DC // 2)

        @block.gpsimd
        def _(pool):
            nc.gpsimd.memset(u[:, :, 0:TAPS - 1], 0.0).then_inc(msk_ok, 1)
            for k in range(4):
                pool.dma_start(ada[:, k, :], w_ada[k]).then_inc(ada_in[k], 16)
            with pool.Fori(1, ADA // 4) as turn:
                for k in range(4):
                    n = turn * 4 + k
                    pool.wait_ge(ada_used, n - 3)
                    pool.dma_start(ada[:, k, :], w_ada[bass.ds(n, 1)].rearrange("a p n -> p (a n)")
                                   ).then_inc(ada_in[k], 16)
            for h in range(HEADS):
                if h >= 2:
                    pool.wait_ge(sb_ok, TT * (h - 1))
                pool.dma_start(toep[:, h % 2, :], toep_d[:, h, :]).then_inc(toep_in[h % 2], 16)
                pool.wait_ge(toep_in[h % 2], 16 * (h // 2 + 1))
                nc.gpsimd.memset(toep[0:CHUNK, h % 2, T - CHUNK:T], MASKED).then_inc(msk_ok, 1)
            pool.wait_ge(m_ok, DC)
            pool.dma_start(keys[:, :, :], keys_d).then_inc(keys_in, 16)
            with pool.Fori(0, T // TB // 2) as it:
                for s in range(2):
                    pool.wait_ge(g_cp, (it * 2 + (s + 1)) * (TB // 4))
                    pool.dma_start(g_d[bass.ds(it * 2 + s, 1)].rearrange("a p n -> p (a n)"),
                                   gb[:, s, :, :].rearrange("p j t -> p (j t)")).then_inc(gw_out[s], 16)
            for s in range(2):
                pool.wait_ge(gw_out[s], 16 * (T // TB // 2))

            def g_load(k, s):
                pool.dma_start(gtile[:, s, :, :, :].rearrange("p b j t -> p b (j t)"),
                               g_d[:, :, bass.ds(k * 4 * TB, 4 * TB)].rearrange("b p n -> p b n")
                               ).then_inc(gt_in[s], 16)

            g_load(0, 0)
            g_load(1, 1)
            with pool.Fori(1, NKEY // 8) as kk:
                for s in range(2):
                    pool.wait_ge(c_mul, kk * 8 + 4 * s)
                    g_load(kk * 2 + s, s)

        def round_unit(act, n, slot):
            act.wait_ge(w_in[slot], 16 * (n // RING + 1) if isinstance(n, int) else n[1])
            nn = n if isinstance(n, int) else n[0]
            if not isinstance(n, int) or n >= RING:
                act.wait_ge(w_used, nn - RING + 1)
            nc.scalar.activation(w_hi[:, slot, :], stage[:, slot, :], ACT.Copy).then_inc(w_round, 1)

        @block.scalar
        def _(act):
            act.dma_start(par[:, :], par_d).then_inc(par_in, 16)
            act.dma_start(const[:, :], const_d).then_inc(par_in, 16)
            act.dma_start(selt[:, :], selt_d).then_inc(selt_in, 16)
            act.wait_ge(par_in, 32)
            nc.scalar.activation(small[:, 0:DC], col("c", 0, DC), ACT.Silu).then_inc(cond_ok, 1)
            act.wait_ge(x_in, 16)
            squares = 0

            def square(src, used):
                nonlocal squares
                if used > 0:
                    act.wait_ge(sq_used, used)
                nc.scalar.activation(sq[:, squares % 2, :], src, ACT.Square).then_inc(sq_ok, 1)
                squares += 1

            for m in range(DC):
                square(x[:, m, :], squares - 1)
            act.wait_ge(ms_ok, 1)
            nc.scalar.activation(rstd, rstd, ACT.Sqrt).then_inc(rt_ok, 1)
            for n in range(3):
                round_unit(act, n, n % RING)
            hi = 0

            def act_round(m, done):
                nonlocal hi
                act.wait_ge(a_pre, done + m + 1)
                nc.scalar.activation(act_hi[:, m, :], tmp[:, m % 2, :], ACT.Copy).then_inc(a_hi, 1)
                hi += 1

            for m in range(DC):
                act_round(m, 0)

            def evac(n):
                pb = UB[n % 4][:, :]
                act.wait_ge(w_used, n + 1)
                if n < QK0:
                    if n % 2 == 0:
                        i = n // 2
                        if i >= 2:
                            act.wait_ge(u_ok, i - 1)
                        nc.scalar.activation(tmp[:, i % 2, :], pb, ACT.Sigmoid).then_inc(sig_ok, 1)
                elif n < V0:
                    nc.scalar.activation(wide[:, n - QK0, :], pb, ACT.Copy).then_inc(qk_ok, 1)
                    square(pb, squares - 1)
                elif n < MIX0:
                    c = n - V0
                    nc.scalar.activation(vtok[:, :, c * P:(c + 1) * P], pb.rearrange("p (t f) -> p t f", t=TT),
                                         ACT.Copy).then_inc(v_ok, 1)

            for n in range(MIX0):
                if n >= 1:
                    evac(n - 1)
                round_unit(act, n + 3, (n + 3) % RING)
                if n == V0:
                    act.wait_ge(ms_ok, 2)
                    nc.scalar.activation(rstd[0:16, :], rstd[0:16, :], ACT.Sqrt).then_inc(rt_ok, 1)
            evac(MIX0 - 1)

            for s in range(HEADS * TT + 3):
                if s < HEADS * TT:
                    n = (s % TT + 1) * P
                    act.wait_ge(sb_ok, s + 1)
                    nc.scalar.activation(sc[:, s % 3, 0:n], sc[:, s % 3, 0:n], ACT.Exp,
                                         bias=small[:, 48 + s % 4:49 + s % 4],
                                         accum_out=small[:, 52 + s % 4:53 + s % 4]).then_inc(e_ok, 1)
                r = s - 2
                if 0 <= r < HEADS * TT:
                    h, q = divmod(r, TT)
                    if h >= 2:
                        act.wait_ge(o_ok, h - 1)
                    act.wait_ge(t_ok, r + 1)
                    n = (q + 1) * P
                    nc.scalar.activation(pt[:, h % 2, 0:q + 1, q * P:(q + 1) * P],
                                         UB[r % 2][:, 0:n].rearrange("p (b q) -> p b q", q=P),
                                         ACT.Copy).then_inc(pt_ok, 1)
                if r in (2 * TT, 4 * TT, 6 * TT):
                    pair = r // (2 * TT) - 1
                    act.wait_ge(o_ok, 2 * pair + 2)
                    nc.scalar.activation(mix_hi[:, CC + pair, :], UB[2 + pair % 2][:, :], ACT.Copy).then_inc(a_hi, 1)
                    hi += 1
            act.wait_ge(o_ok, HEADS)
            nc.scalar.activation(mix_hi[:, CC + 3, :], UB[3][:, :], ACT.Copy).then_inc(a_hi, 1)
            hi += 1

            def mix_evac(n):
                kind = MIX[n - MIX0]
                if kind[0] == "gate":
                    _, m, br = kind
                    act.wait_ge(w_used, n + 1)
                    if m >= 2:
                        act.wait_ge(m_ok, m - 1)
                    nc.scalar.activation(gate[:, 2 * (m % 2) + br, :], UB[n % 4][:, :], ACT.Sigmoid).then_inc(sig_ok, 1)

            for n in range(MIX0, WOUT0):
                if n > MIX0:
                    mix_evac(n - 1)
                round_unit(act, n + 3, (n + 3) % RING)
                if n == MIX0 + 1:
                    for i in range(CC):
                        act.wait_ge(y_ok, i + 1)
                        square(y[:, i, :], squares - 1)
                    act.wait_ge(ms_ok, 4)
                    nc.scalar.activation(rstd, rstd, ACT.Sqrt).then_inc(rt_ok, 1)
                if n == MIX0 + 3:
                    for i in range(CC):
                        act.wait_ge(y_nrm, i + 1)
                        nc.scalar.activation(y[:, i, :], y[:, i, :], ACT.Silu, scale=col("ln_g", i),
                                             bias=col("ln_b", i)).then_inc(y_act, 1)
                        act.wait_ge(y_act, i + 1)
                        nc.scalar.activation(mix_hi[:, i, :], y[:, i, :], ACT.Copy).then_inc(a_hi, 1)
                        hi += 1

            def merged_round(m):
                nonlocal hi
                if m == 0:
                    act.wait_ge(w_used, WOUT0 - 1)
                act.wait_ge(m_ok, m + 1)
                nc.scalar.activation(act_hi[:, m, :], wide[:, m, :], ACT.Copy).then_inc(a_hi, 1)
                hi += 1

            for m in range(DC):
                merged_round(m)
            for n in range(WOUT0, WQ0):
                m = n - WOUT0 - 1
                if m >= 0:
                    act.wait_ge(x2_ok, m + 1)
                    square(x[:, m, :], squares - 1)
                round_unit(act, n + 3, (n + 3) % RING)
            act.wait_ge(x2_ok, DC)
            square(x[:, DC - 1, :], squares - 1)
            act.wait_ge(ms_ok, 5)
            nc.scalar.activation(rstd, rstd, ACT.Sqrt).then_inc(rt_ok, 1)
            for m in range(DC):
                act_round(m, DC)

            def wq_evac(c):
                n = WQ0 + c
                act.wait_ge(w_used, n + 1)
                if c >= 2:
                    act.wait_ge(ks_ok, c - 1)
                nc.scalar.activation(qf[:, c % 2, :], UB[n % 4][:, :], ACT.Copy).then_inc(qf_ok, 1)

            def ks_evac(c):
                act.wait_ge(ks_ok, c + 1)
                nc.scalar.activation(scores[:, :, c, :], XB[c % 2][:, :].rearrange("p (t k) -> p t k", t=TT),
                                     ACT.Copy).then_inc(sc_ok, 1)

            for c in range(2 * PH):
                if c >= 1:
                    wq_evac(c - 1)
                round_unit(act, WQ0 + c + 3, (WQ0 + c + 3) % RING) if WQ0 + c + 3 < FRONT else None
                if c >= 2:
                    ks_evac(c - 2)
            wq_evac(2 * PH - 1)
            ks_evac(2 * PH - 2)
            ks_evac(2 * PH - 1)
            for n in range(FRONT, FRONT + 3):
                round_unit(act, n, n % RING)

            for tt in range(TT):
                act.wait_ge(tk_ok, tt + 1)
                v = top[:, tt, :, :].rearrange("p h k -> p (h k)")
                nc.scalar.activation(v, v, ACT.Exp).then_inc(te_ok, 1)
            for tt in range(TT):
                act.wait_ge(ijt_ok, tt + 1)
                nc.scalar.activation(ijt[:, :, tt * P:(tt + 1) * P], XB[tt % 2][:, 0:3 * P].rearrange(
                    "p (c t) -> p c t", c=3), ACT.Copy).then_inc(ijt_cp, 1)

            def g_evac(it, s, b):
                k = it * (2 * TB // 4) + (s * (TB // 4) + b)
                act.wait_ge(g_ok, k + 1)
                nc.scalar.activation(gb[:, s, :, 4 * b:4 * b + 4].rearrange("p j t -> p t j"),
                                     bank[b % 4][:, :].rearrange("p (t j) -> p t j", t=4), ACT.Copy).then_inc(g_cp, 1)

            def g_pair(it, first):
                for s in range(2):
                    if not first:
                        act.wait_ge(gw_out[s], it * 16)
                    for b in range(TB // 4):
                        g_evac(it, s, b)

            g_pair(0, True)
            with act.Fori(1, T // TB // 2) as it:
                g_pair(it, False)

            def group(g, last):
                for k in range(2 * SLABS):
                    n0 = g * (2 * SLABS) + FRONT
                    q = g * SLABS + (k - 1)
                    if 1 <= k <= SLABS:
                        s = k - 1
                        act.wait_ge(w_used, n0 + k)
                        act.wait_ge(c_mul, q + 3)
                        nc.scalar.activation(ga[:, s % 2, :], UB[s % 4][:, :], ACT.Gelu).then_inc(ge_ok, 1)
                    if not (last and k + 3 >= 2 * SLABS):
                        slot = (k + 3) % RING
                        turns = g * 4 + (FRONT // RING + (k + 3) // RING + 1)
                        round_unit(act, (n0 + (k + 3), turns * 16), slot)
                    if 1 <= k <= SLABS:
                        s = k - 1
                        if s == 0:
                            act.wait_ge(w_used, n0)
                        act.wait_ge(c_mul, q + 5)
                        nc.scalar.activation(mix_hi[:, s, :], cf[:, s % 2, :], ACT.Copy).then_inc(c_hi, 1)

            with act.Fori(0, GROUPS - 1) as g:
                group(g, False)
            group(GROUPS - 1, True)

        @block.vector
        def _(dve):
            count = {"step": 0}

            def link(ins):
                count["step"] += 1
                ins.then_inc(step, 1)
                dve.wait_ge(step, count["step"])

            def mark(ins):
                count["step"] += 1
                ins.then_inc(step, 1)
                return count["step"]

            def split_unit(n, slot):
                dve.wait_ge(w_round, n + 1)
                nc.vector.tensor_tensor(w_lo[:, slot, :], stage[:, slot, :], w_hi[:, slot, :].bitcast(F32),
                                        ALU.subtract).then_inc(w_split, 1)

            lo = 0

            def lo_part(dst, src, hi_ap):
                nonlocal lo
                dve.wait_ge(a_hi, lo + 1)
                nc.vector.tensor_tensor(dst, src, hi_ap.bitcast(F32), ALU.subtract).then_inc(a_lo, 1)
                lo += 1

            dve.wait_ge(par_in, 32)
            link(nc.vector.tensor_scalar(small[:, 40:41], col("qg"), HD ** -0.5, None, ALU.mult))

            def norm_scale(width):
                count["ms"] = count.get("ms", 0) + 1
                nc.vector.tensor_scalar(rstd, STAT[:, :], 1.0 / width, EPS, ALU.mult, ALU.add).then_inc(ms_ok, 1)
                dve.wait_ge(rt_ok, count["ms"])
                link(nc.vector.reciprocal(rstd, rstd))

            def modulated(a0, b0, w_first):
                for m in range(DC + 1):
                    if m < DC:
                        if m >= 2:
                            dve.wait_ge(a_lo, lo)
                        link(nc.vector.tensor_tensor(tmp[:, m % 2, :], x[:, m, :], rstd, ALU.mult))
                        nc.vector.tensor_scalar(tmp[:, m % 2, :], tmp[:, m % 2, :], small[:, a0 + m:a0 + m + 1],
                                                mod[:, b0 + m:b0 + m + 1], ALU.mult, ALU.add).then_inc(a_pre, 1)
                    if m >= 1:
                        lo_part(act_lo[:, m - 1, :], tmp[:, (m - 1) % 2, :], act_hi[:, m - 1, :])
                    if m in (3, 5) and w_first is not None:
                        split_unit(w_first + (m - 3) // 2, (w_first + (m - 3) // 2) % RING)

            dve.wait_ge(sq_used, DC)
            norm_scale(D)
            dve.wait_ge(ada_used, ADA_FIRST)
            link(nc.vector.tensor_tensor(mod[:, 0:ADA_FIRST], MODB[:, 0:ADA_FIRST], col("b_ada", 0, ADA_FIRST), ALU.add))
            link(nc.vector.tensor_scalar(small[:, 8:16], mod[:, DC:2 * DC], 1.0, None, ALU.add))
            link(nc.vector.tensor_tensor(small[:, 8:16], small[:, 8:16], col("g1", 0, DC), ALU.mult))
            modulated(8, 0, 0)

            def taps():
                for pair in range(2):
                    marks = {}
                    for w in range(TAPS):
                        for i in (2 * pair, 2 * pair + 1):
                            def one(w=w, i=i, marks=marks):
                                src = u[:, i, w:w + T]
                                wt = col("dw", i * TAPS + w)
                                if w == 0:
                                    dve.wait_ge(u_ok, 2 * pair + 2)
                                    if i == 0:
                                        dve.wait_ge(msk_ok, 1)
                                    ins = nc.vector.tensor_scalar(y[:, i, :], src, wt, col("conv_b", i),
                                                                  ALU.mult, ALU.add)
                                else:
                                    dve.wait_ge(step, marks[i])
                                    ins = nc.vector.scalar_tensor_tensor(out=y[:, i, :], in0=src, scalar=wt,
                                                                         in1=y[:, i, :], op0=ALU.mult, op1=ALU.add)
                                marks[i] = mark(ins)
                            yield one

            tap = taps()

            def conv(k):
                for _ in range(k):
                    f = next(tap, None)
                    if f:
                        f()

            for n in range(MIX0):
                split_unit(n + 2, (n + 2) % RING)
                j = n - 1
                if 0 <= j < QK0 and j % 2 == 1:
                    i = j // 2
                    dve.wait_ge(w_used, j + 1)
                    dve.wait_ge(sig_ok, i + 1)
                    nc.vector.tensor_tensor(u[:, i, TAPS - 1:], tmp[:, i % 2, :], UB[j % 4][:, :],
                                            ALU.mult).then_inc(u_ok, 1)
                if n == V0:
                    dve.wait_ge(sq_used, 2 * DC)
                    count["ms"] += 1
                    nc.vector.tensor_scalar(rstd[0:16, :], STAT[0:16, :], 1.0 / HD, EPS, ALU.mult, ALU.add
                                            ).then_inc(ms_ok, 1)
                    dve.wait_ge(ada_used, ADA)
                    link(nc.vector.tensor_tensor(mod[:, ADA_FIRST:], MODB[:, ADA_FIRST:ADA],
                                                 col("b_ada", ADA_FIRST, ADA - ADA_FIRST), ALU.add))
                    link(nc.vector.tensor_scalar(small[:, 16:24], mod[:, 4 * DC:5 * DC], 1.0, None, ALU.add))
                    link(nc.vector.tensor_tensor(small[:, 16:24], small[:, 16:24], col("g2", 0, DC), ALU.mult))
                    dve.wait_ge(rt_ok, 2)
                    nc.vector.reciprocal(rstd[0:16, :], rstd[0:16, :]).then_inc(ms_ok, 1)
                if n > V0:
                    for m in range((n - V0 - 1) * 3, min((n - V0) * 3, 8)):
                        dve.wait_ge(rb_ok, m + 1)
                        dve.wait_ge(qk_ok, m + 1)
                        nc.vector.scalar_tensor_tensor(out=wide[:, m, :], in0=wide[:, m, :],
                                                       scalar=small[:, 40:41] if m < 4 else col("kg"),
                                                       in1=XB[m % 2][:, :], op0=ALU.mult, op1=ALU.mult
                                                       ).then_inc(qkn_ok, 1)
                if n >= 4:
                    conv(5 if n < V0 else 3)

            def o_lo(pair):
                nonlocal lo
                dve.wait_ge(a_hi, lo + 1)
                nc.vector.tensor_tensor(mix_lo[:, CC + pair, :], UB[2 + pair % 2][:, :],
                                        mix_hi[:, CC + pair, :].bitcast(F32), ALU.subtract).then_inc(a_lo, 1)
                lo += 1

            for s in range(HEADS * TT + 1):
                if s < HEADS * TT:
                    h, q = divmod(s, TT)
                    n = (q + 1) * P
                    if s >= 3:
                        dve.wait_ge(t_ok, s - 2)
                    dve.wait_ge(s_ok, s + 1)
                    dve.wait_ge(msk_ok, h + 2)
                    link(nc.vector.tensor_tensor_reduce(sc[:, s % 3, 0:n], XB[s % 2][:, 0:n],
                                                        toep[:, h % 2, T - n:T], 1.0, LOWEST, ALU.add, ALU.max,
                                                        small[:, 44 + s % 4:45 + s % 4]))
                    nc.vector.tensor_scalar(small[:, 48 + s % 4:49 + s % 4], small[:, 44 + s % 4:45 + s % 4], -1.0,
                                            None, ALU.mult).then_inc(sb_ok, 1)
                r = s - 1
                if r >= 0:
                    n = (r % TT + 1) * P
                    dve.wait_ge(e_ok, r + 1)
                    link(nc.vector.reciprocal(small[:, 56 + r % 4:57 + r % 4], small[:, 52 + r % 4:53 + r % 4]))
                    nc.vector.tensor_scalar(sc[:, r % 3, 0:n], sc[:, r % 3, 0:n], small[:, 56 + r % 4:57 + r % 4],
                                            None, ALU.mult).then_inc(p_ok, 1)
                conv(2)
                if s >= 2 * TT + 4 and (s - 4) % (2 * TT) == 0:
                    o_lo((s - 4) // (2 * TT) - 1)
            conv(200)

            def merge(m):
                n = MIX0 + MIX.index(("out", m))
                dve.wait_ge(w_used, n + 1)
                dve.wait_ge(sig_ok, CC + 2 * m + 2)
                a = mark(nc.vector.tensor_tensor(gate[:, 2 * (m % 2), :], gate[:, 2 * (m % 2), :], UB[n % 4][:, :], ALU.mult))
                b = mark(nc.vector.tensor_tensor(gate[:, 2 * (m % 2) + 1, :], gate[:, 2 * (m % 2) + 1, :], XB[m % 2][:, :],
                                                 ALU.mult))
                dve.wait_ge(step, b)
                nc.vector.tensor_tensor(wide[:, m, :], gate[:, 2 * (m % 2), :], gate[:, 2 * (m % 2) + 1, :],
                                        ALU.add).then_inc(m_ok, 1)

            split_unit(MIX0 + 2, (MIX0 + 2) % RING)
            dve.wait_ge(step, count["step"])
            nc.vector.memset(small[:, 60:61], 0.0).then_inc(conv_ok, 1)
            o_lo(3)
            dve.wait_ge(y_sum, 1)
            link(nc.vector.tensor_scalar(rstd, XB[0][:, :], 1.0 / 512, None, ALU.mult))
            for i in range(CC):
                nc.vector.tensor_tensor(y[:, i, :], y[:, i, :], rstd, ALU.subtract).then_inc(y_ok, 1)
            split_unit(MIX0 + 3, (MIX0 + 3) % RING)
            dve.wait_ge(sq_used, 2 * DC + CC)
            norm_scale(512)
            split_unit(MIX0 + 4, (MIX0 + 4) % RING)
            for i in range(CC):
                nc.vector.tensor_tensor(y[:, i, :], y[:, i, :], rstd, ALU.mult).then_inc(y_nrm, 1)
            for i in range(CC):
                lo_part(mix_lo[:, i, :], y[:, i, :], mix_hi[:, i, :])
            for n in range(MIX0 + 3, WOUT0):
                split_unit(n + 2, (n + 2) % RING)
                if MIX[n - 1 - MIX0][0] == "out":
                    merge(MIX[n - 1 - MIX0][1])
            for m in range(DC - 1):
                lo_part(act_lo[:, m, :], wide[:, m, :], act_hi[:, m, :])
            merge(DC - 1)
            lo_part(act_lo[:, DC - 1, :], wide[:, DC - 1, :], act_hi[:, DC - 1, :])

            for n in range(WOUT0, WQ0 + 1):
                if n < WQ0:
                    split_unit(n + 2, (n + 2) % RING)
                m = n - 1 - WOUT0
                if m >= 0:
                    dve.wait_ge(w_used, n)
                    nc.vector.scalar_tensor_tensor(out=x[:, m, :], in0=UB[(n - 1) % 4][:, :],
                                                   scalar=mod[:, 2 * DC + m:2 * DC + m + 1], in1=x[:, m, :],
                                                   op0=ALU.mult, op1=ALU.add).then_inc(x2_ok, 1)
            dve.wait_ge(sq_used, 3 * DC + CC)
            norm_scale(D)
            modulated(16, 3 * DC, None)

            def topk(tt, h):
                if h == 0 and tt == 0:
                    dve.wait_ge(a_lo, lo)
                dve.wait_ge(sc_ok, 2 * h + 2)
                last = {}
                for part in range(5):
                    for p in range(2):
                        s = scores[:, tt, 2 * h + p, :]
                        v, ix = sv[:, tt, 2 * h + p, :], si[:, tt, 2 * h + p, :]
                        if part:
                            dve.wait_ge(step, last[p])
                        if part == 0:
                            ins = nc.vector.max(v[:, 0:8], s)
                        elif part == 1:
                            ins = nc.vector.max_index(ix[:, 0:8], v[:, 0:8], s)
                        elif part == 2:
                            ins = nc.vector.match_replace(mr[:, p, :], v[:, 0:8], s, LOWEST)
                        elif part == 3:
                            ins = nc.vector.max(v[:, 8:16], mr[:, p, :])
                        else:
                            ins = nc.vector.max_index(ix[:, 8:16], v[:, 8:16], mr[:, p, :])
                        last[p] = mark(ins)
                a = sv[:, tt, 2 * h, :].rearrange("p (k o) -> p k o", o=1).to_broadcast([P, TOPK, TOPK])
                b = sv[:, tt, 2 * h + 1, :].rearrange("p (o k) -> p o k", o=1).to_broadcast([P, TOPK, TOPK])
                link(nc.vector.tensor_tensor(cand.rearrange("p (a b) -> p a b", b=TOPK), a, b, ALU.add))
                link(nc.vector.max(top[:, tt, h, 0:8], cand))
                mark(nc.vector.max_index(pos[:, tt, h, 0:8], top[:, tt, h, 0:8], cand))
                link(nc.vector.match_replace(cand2, top[:, tt, h, 0:8], cand, LOWEST))
                link(nc.vector.max(top[:, tt, h, 8:16], cand2))
                link(nc.vector.max_index(pos[:, tt, h, 8:16], top[:, tt, h, 8:16], cand2))

            jobs = [(tt, h) for h in range(PH) for tt in range(TT)]
            for c in range(2 * PH):
                if WQ0 + c + 2 < FRONT:
                    split_unit(WQ0 + c + 2, (WQ0 + c + 2) % RING)
                if c >= 4:
                    for _ in range(2):
                        topk(*jobs.pop(0))
            while jobs:
                topk(*jobs.pop(0))
            for n in range(FRONT, FRONT + 2):
                split_unit(n, n % RING)
            link(nc.vector.tensor_copy(small[:, 80:112].rearrange("p (t h) -> p t h", t=TT), top[:, :, :, 0]))
            for tt in range(TT):
                nc.vector.tensor_tensor(top[:, tt, :, :], top[:, tt, :, :],
                                        small[:, 80 + PH * tt:80 + PH * tt + PH].rearrange(
                                            "p (h o) -> p h o", o=1).to_broadcast([P, PH, TOPK]), ALU.subtract
                                        ).then_inc(tk_ok, 1)
            eq = hot16.rearrange("p (c r) -> p c r", r=TOPK)
            eq4 = hot16.rearrange("p (h k r) -> p h k r", h=PH, k=TOPK)
            for tt in range(TT):
                pv = pos[:, tt, :, :].rearrange("p h k -> p (h k)")
                mark(nc.vector.tensor_scalar(ranku[:, 0, :], pv, 4, None, ALU.logical_shift_right))
                mark(nc.vector.tensor_scalar(ranku[:, 1, :], pv, 15, None, ALU.bitwise_and))
                link(nc.vector.tensor_copy(sif, si[:, tt, :, :].rearrange("p c k -> p (c k)")))
                link(nc.vector.tensor_copy(rank[:, :, :], ranku[:, :, :]))
                for half in range(2):
                    if half == 0 and tt:
                        dve.wait_ge(ijt_ok, tt)
                    link(nc.vector.tensor_tensor(eq, rank[:, half, :].rearrange("p (c o) -> p c o", o=1).to_broadcast(
                        [P, P, TOPK]), iota16.rearrange("p (o r) -> p o r", o=1).to_broadcast([P, P, TOPK]),
                        ALU.is_equal))
                    six = sif.rearrange("p (h two r) -> p h two r", h=PH, two=2)[:, :, half:half + 1, :]
                    link(nc.vector.tensor_tensor(eq4, eq4, six.to_broadcast([P, PH, TOPK, TOPK]), ALU.mult))
                    link(nc.vector.tensor_reduce(ijw[:, half, :], eq, AX.X, ALU.add))
                dve.wait_ge(te_ok, tt + 1)
                e = top[:, tt, :, :]
                link(nc.vector.tensor_reduce(small[:, 64:72], e, AX.X, ALU.add))
                link(nc.vector.reciprocal(small[:, 72:80], small[:, 64:72]))
                nc.vector.tensor_tensor(ijw[:, 2, :].rearrange("p (h k) -> p h k", h=PH), e,
                                        small[:, 72:80].rearrange("p (h o) -> p h o", o=1).to_broadcast(
                                            [P, PH, TOPK]), ALU.mult).then_inc(ijw_ok, 1)
                dve.wait_ge(ijw_ok, tt + 1)

            dve.wait_ge(ijt_cp, TT)

            def hots(it, first):
                for t in range(2 * TB):
                    k = it * (2 * TB) + t
                    if not (first and t < 8):
                        if t % 4 == 0:
                            dve.wait_ge(g_ok, it * (2 * TB // 4) + (t // 4 - 1))
                    icol, jcol, wcol = (ijt[:, c, bass.ds(k, 1)] for c in range(3))
                    nc.vector.tensor_scalar(hot[:, t % 8, 0, :], iota, icol, None, ALU.is_equal).then_inc(hot_ok, 1)
                    nc.vector.tensor_scalar(hot[:, t % 8, 1, :], iota, jcol, wcol, ALU.is_equal, ALU.mult
                                            ).then_inc(hot_ok, 1)

            hots(0, True)
            with dve.Fori(1, T // TB // 2) as it:
                hots(it, False)

            dve.wait_ge(g_cp, T // 4)
            dve.wait_ge(gw_out[0], 16 * (T // TB // 2))
            dve.wait_ge(gw_out[1], 16 * (T // TB // 2))
            for m in range(4):
                nc.vector.memset(wide[:, 2 * m:2 * m + 2, :], 0.0).then_inc(acc_ok, 1)
            for m in range(4):
                nc.vector.memset(cf[:, m // 2, m % 2 * 256:m % 2 * 256 + 256], 0.0).then_inc(c_mul, 1)

            for m in range(2):
                nc.vector.memset(fin[:, m, :], 0.0).then_inc(c_lo, 1)

            def group(g, last):
                for k in range(2 * SLABS):
                    n0 = g * (2 * SLABS) + FRONT
                    if not (last and k + 2 >= 2 * SLABS):
                        split_unit(n0 + (k + 2), (k + 2) % RING)
                    if 1 <= k <= SLABS:
                        s = k - 1
                        q = g * SLABS + s
                        if s % 4 == 0:
                            dve.wait_ge(gt_in[s // 4], g * 16 + 16)
                        dve.wait_ge(ge_ok, q + 1)
                        dve.wait_ge(c_lo, q + 1)
                        nc.vector.tensor_tensor(cf[:, s % 2, :].rearrange("p (b t) -> p b t", t=TB),
                                                ga[:, s % 2, :].rearrange("p (b t) -> p b t", t=TB),
                                                gtile[:, s // 4, :, s % 4, :], ALU.mult).then_inc(c_mul, 1)
                        dve.wait_ge(c_hi, q + 1)
                        nc.vector.tensor_tensor(mix_lo[:, s, :], cf[:, s % 2, :], mix_hi[:, s, :].bitcast(F32),
                                                ALU.subtract).then_inc(c_lo, 1)
                    if k in (11, 15):
                        hf = (k - 11) // 4
                        for m in range(4):
                            if m < 3:
                                dve.wait_ge(v_part, g * 6 + (3 * hf + m + 1))
                            else:
                                dve.wait_ge(w_used, n0 + (k + 1))
                            nc.vector.tensor_tensor(wide[:, 4 * hf + m, :], wide[:, 4 * hf + m, :], bank[m][:, :],
                                                    ALU.add).then_inc(acc_ok, 1)

            with dve.Fori(0, GROUPS - 1) as g:
                group(g, False)
            group(GROUPS - 1, True)
            dve.wait_ge(acc_ok, 4 + 8 * GROUPS)
            for m in range(DC):
                if m >= 2:
                    dve.wait_ge(out_in[m % 2], 16 * (m // 2))
                nc.vector.scalar_tensor_tensor(out=fin[:, m % 2, :], in0=wide[:, m, :],
                                               scalar=mod[:, 5 * DC + m:5 * DC + m + 1], in1=x[:, m, :],
                                               op0=ALU.mult, op1=ALU.add).then_inc(fin_ok, 1)

        @block.tensor
        def _(pe):
            sums = 0

            def ada_unit(n):
                pe.wait_ge(ada_in[n % 4], 16 * (n // 4 + 1))
                for dc in range(DC):
                    last = nc.tensor.matmul(MODB[:, n:n + 1], ada[:, n % 4, dc * P:(dc + 1) * P],
                                            small[:, dc:dc + 1], start=(dc == 0), stop=(dc == DC - 1))
                last.then_inc(ada_used, 1)

            def sum_squares(m, n, lhs=None, out=None):
                nonlocal sums
                pe.wait_ge(sq_ok, sums + 1)
                nc.tensor.matmul(STAT[:, :] if out is None else out, ones if lhs is None else lhs,
                                 sq[:, sums % 2, :], start=(m == 0), stop=(m == n - 1)).then_inc(sq_used, 1)
                sums += 1

            def product(out, slot, dcs, rhs_hi, rhs_lo, col0=0):
                for i, dc in enumerate(dcs):
                    w = slice(col0 + dc * P, col0 + (dc + 1) * P)
                    nc.tensor.matmul(out, w_hi[:, slot, w], rhs_hi[:, dc, :], start=(i == 0), stop=False)
                    nc.tensor.matmul(out, w_hi[:, slot, w], rhs_lo[:, dc, :], start=False, stop=False)
                    last = nc.tensor.matmul(out, w_lo[:, slot, w], rhs_hi[:, dc, :], start=False,
                                            stop=(i == len(dcs) - 1))
                return last

            def unit(n, rhs_hi, rhs_lo, first_lo=None):
                pe.wait_ge(w_split, n + 1)
                if n >= 4:
                    pe.wait_ge(*sums_read(n - 4))
                if first_lo is None:
                    product(UB[n % 4][:, :], n % RING, range(DC), rhs_hi, rhs_lo).then_inc(w_used, 1)
                    return
                for dc in range(DC):
                    pe.wait_ge(a_lo, first_lo + dc + 1)
                    w = slice(dc * P, (dc + 1) * P)
                    nc.tensor.matmul(UB[n % 4][:, :], w_hi[:, n % RING, w], rhs_hi[:, dc, :], start=(dc == 0), stop=False)
                    nc.tensor.matmul(UB[n % 4][:, :], w_hi[:, n % RING, w], rhs_lo[:, dc, :], start=False, stop=False)
                    last = nc.tensor.matmul(UB[n % 4][:, :], w_lo[:, n % RING, w], rhs_hi[:, dc, :], start=False,
                                            stop=(dc == DC - 1))
                last.then_inc(w_used, 1)

            pe.wait_ge(par_in, 32)
            for m in range(DC):
                sum_squares(m, DC)
            pe.wait_ge(cond_ok, 1)
            for n in range(ADA_FIRST):
                ada_unit(n)
            for n in range(V0):
                unit(n, act_hi, act_lo, 0 if n == 0 else None)
                ada_unit(ADA_FIRST + 2 * n)
                ada_unit(ADA_FIRST + 2 * n + 1)
                if n > QK0:
                    sum_squares(n - 1 - QK0, DC, sel[:, n - 1 - QK0, :], STAT[0:16, :])
            sum_squares(DC - 1, DC, sel[:, DC - 1, :], STAT[0:16, :])
            pe.wait_ge(selt_in, 16)
            for n in range(V0, MIX0):
                pe.wait_ge(w_split, n + 1)
                pe.wait_ge(*sums_read(n - 4))
                for tt in range(TT):
                    o = UB[n % 4][:, tt * P:(tt + 1) * P]
                    for dc in range(DC):
                        w = slice(dc * P, (dc + 1) * P)
                        t = slice(tt * P, (tt + 1) * P)
                        nc.tensor.matmul(o, act_hi[:, dc, t], w_hi[:, n % RING, w], start=(dc == 0), stop=False)
                        nc.tensor.matmul(o, act_hi[:, dc, t], w_lo[:, n % RING, w], start=False, stop=False)
                        last = nc.tensor.matmul(o, act_lo[:, dc, t], w_hi[:, n % RING, w], start=False,
                                                stop=(dc == DC - 1))
                last.then_inc(w_used, 1)
                if n > V0:
                    for m in range((n - V0 - 1) * 3, min((n - V0) * 3, 8)):
                        if m == 0:
                            pe.wait_ge(ms_ok, 3)
                        if m >= 2:
                            pe.wait_ge(qkn_ok, m - 1)
                        nc.tensor.matmul(XB[m % 2][:, :], selt[:, m * P:(m + 1) * P], rstd[0:16, :],
                                         start=True, stop=True).then_inc(rb_ok, 1)

            pe.wait_ge(qkn_ok, 8)
            pe.wait_ge(v_ok, 4)
            for s in range(HEADS * TT + 3):
                if s < HEADS * TT:
                    h, q = divmod(s, TT)
                    base = HD * (h % 2)
                    n = (q + 1) * P
                    if s >= 2:
                        pe.wait_ge(sb_ok, s - 1)
                    nc.tensor.matmul(XB[s % 2][:, 0:n], wide[base:base + HD, h // 2, q * P:(q + 1) * P],
                                     wide[base:base + HD, 4 + h // 2, 0:n], start=True, stop=True).then_inc(s_ok, 1)
                r = s - 2
                if 0 <= r < HEADS * TT:
                    pe.wait_ge(p_ok, r + 1)
                    if r >= 2:
                        pe.wait_ge(pt_ok, r - 1)
                    for b in range(r % TT + 1):
                        last = nc.tensor.transpose(UB[r % 2][:, b * P:(b + 1) * P], sc[:, r % 3, b * P:(b + 1) * P], ident)
                    last.then_inc(t_ok, 1)
                r = s - 3
                if r >= 0 and r % TT == TT - 1:
                    h = r // TT
                    pair = h // 2
                    if pair >= 2 and h % 2 == 0:
                        pe.wait_ge(a_lo, DC + pair - 1)
                    pe.wait_ge(pt_ok, r + 1)
                    base = HD * (h % 2)
                    for kb in range(TT):
                        last = nc.tensor.matmul(UB[2 + pair % 2][base:base + HD, kb * P:T],
                                                vtok[:, kb, h * HD:(h + 1) * HD], pt[:, h % 2, kb, kb * P:T],
                                                start=(kb == 0), stop=(kb == TT - 1))
                    last.then_inc(o_ok, 1)

            pe.wait_ge(pt_ok, HEADS * TT)
            pe.wait_ge(sb_ok, HEADS * TT)

            def mix_unit(n):
                kind = MIX[n - MIX0]
                if kind[0] == "gate":
                    if n - MIX0 < 4 and n % 4 >= 2:
                        pe.wait_ge(a_lo, DC + CC)
                    unit(n, act_hi, act_lo)
                    return
                m = kind[1]
                pe.wait_ge(w_split, n + 1)
                pe.wait_ge(*sums_read(n - 4))
                if m >= 2:
                    pe.wait_ge(m_ok, m - 1)
                if m == 0:
                    pe.wait_ge(a_lo, DC + 2 * CC)
                product(UB[n % 4][:, :], n % RING, range(CC), mix_hi, mix_lo)
                product(XB[m % 2][:, :], n % RING, range(CC, 2 * CC), mix_hi, mix_lo).then_inc(w_used, 1)

            pe.wait_ge(conv_ok, 1)
            mix_unit(MIX0)
            for i in range(CC):
                last = nc.tensor.matmul(XB[0][:, :], ones, y[:, i, :], start=(i == 0), stop=(i == CC - 1))
            last.then_inc(y_sum, 1)
            mix_unit(MIX0 + 1)
            for i in range(CC):
                sum_squares(i, CC)
            for n in range(MIX0 + 2, WOUT0):
                mix_unit(n)
            merged_lo = DC + 2 * CC
            for n in range(WOUT0, WQ0):
                unit(n, act_hi, act_lo, merged_lo if n == WOUT0 else None)
                if n > WOUT0:
                    sum_squares(n - 1 - WOUT0, DC)
            sum_squares(DC - 1, DC)

            h2_lo = merged_lo + DC

            def key_scores(c):
                pe.wait_ge(qf_ok, c + 1)
                if c >= 2:
                    pe.wait_ge(sc_ok, c - 1)
                for tt in range(TT):
                    last = nc.tensor.matmul(XB[c % 2][:, tt * P:(tt + 1) * P], qf[:, c % 2, tt * P:(tt + 1) * P],
                                            keys[:, c, :], start=True, stop=True)
                last.then_inc(ks_ok, 1)

            for c in range(2 * PH):
                n = WQ0 + c
                unit(n, act_hi, act_lo, h2_lo if c == 0 else None)
                if c == 0:
                    pe.wait_ge(keys_in, 16)
                if c >= 1:
                    key_scores(c - 1)
            key_scores(2 * PH - 1)
            pe.wait_ge(sc_ok, 2 * PH)
            for tt in range(TT):
                pe.wait_ge(ijw_ok, tt + 1)
                if tt >= 2:
                    pe.wait_ge(ijt_cp, tt - 1)
                for c in range(3):
                    last = nc.tensor.transpose(XB[tt % 2][:, c * P:(c + 1) * P], ijw[:, c, :], ident)
                last.then_inc(ijt_ok, 1)
            pe.wait_ge(ijt_cp, TT)

            def g_tokens(it, first):
                for t in range(2 * TB):
                    b = t // 4
                    if t % 4 == 0 and not (first and b < 4):
                        pe.wait_ge(g_cp, it * (2 * TB // 4) + (b - 3))
                    pe.wait_ge(hot_ok, it * (4 * TB) + (2 * t + 2))
                    last = nc.tensor.matmul(bank[b % 4][:, (t % 4) * P:(t % 4 + 1) * P], hot[:, t % 8, 0, :],
                                            hot[:, t % 8, 1, :], start=True, stop=True)
                    if t % 4 == 3:
                        last.then_inc(g_ok, 1)

            g_tokens(0, True)
            with pe.Fori(1, T // TB // 2) as it:
                g_tokens(it, False)
            pe.wait_ge(g_cp, T // 4)

            def group(g):
                n0 = g * (2 * SLABS) + FRONT
                for s in range(SLABS):
                    pe.wait_ge(w_split, n0 + (s + 1))
                    pe.wait_ge(c_mul, g * SLABS + (s + 1))
                    product(UB[s % 4][:, :], s % RING, range(DC), act_hi, act_lo).then_inc(w_used, 1)
                for hf in range(2):
                    for sp_ in range(4):
                        k = SLABS + 4 * hf + sp_
                        slot = k % RING
                        pe.wait_ge(w_split, n0 + (k + 1))
                        if hf == 0:
                            pe.wait_ge(c_lo, g * SLABS + (2 * sp_ + 4))
                        for m in range(4):
                            if sp_ == 0:
                                pe.wait_ge(acc_ok, g * 8 + (4 * hf + m + 1))
                            for half in range(2):
                                s = 2 * sp_ + half
                                w = slice(512 * half + m * P, 512 * half + (m + 1) * P)
                                first, final = s == 0, s == SLABS - 1
                                nc.tensor.matmul(bank[m][:, :], w_hi[:, slot, w], mix_hi[:, s, :], start=first, stop=False)
                                nc.tensor.matmul(bank[m][:, :], w_hi[:, slot, w], mix_lo[:, s, :], start=False, stop=False)
                                last = nc.tensor.matmul(bank[m][:, :], w_lo[:, slot, w], mix_hi[:, s, :], start=False,
                                                        stop=final)
                            if sp_ == 3 and m < 3:
                                last.then_inc(v_part, 1)
                        last.then_inc(w_used, 1)

            with pe.Fori(0, GROUPS) as g:
                group(g)


def layouts(i):
    f = lambda a: np.ascontiguousarray(np.asarray(a))

    def units(w):
        k, n = w.shape
        return w.reshape(k // P, P, n // P, P).transpose(2, 1, 0, 3).reshape(n // P, P, k)

    def cols(v):
        return np.asarray(v).reshape(-1, P).T

    w = {k: np.asarray(v) for k, v in i.items()}
    w_in = units(w["w_in"][0])
    w_mix = np.concatenate([units(w["w_conv_out"][0]), units(w["w_attn_out"][0])], axis=2)
    order = []
    for b in range(CC):
        order += [w_in[CC + b], w_in[b]]
    order += [w_in[8 + m] for m in range(12)]
    for kind in MIX:
        order.append(w_in[20 + DC * kind[2] + kind[1]] if kind[0] == "gate" else w_mix[kind[1]])
    order += list(units(w["w_out"][0])) + list(units(w["peer_wq"][0]))
    dw = w["conv_dw"][0].reshape(TAPS, CC, P).transpose(2, 1, 0).reshape(P, CC * TAPS)
    par = np.concatenate([cols(w["c"][0]), cols(w["b_ada"][0]), cols(w["norm1_g"][0]), cols(w["norm2_g"][0]), dw,
                          cols(w["conv_b"][0]), cols(w["conv_ln_g"][0]), cols(w["conv_ln_b"][0]),
                          np.tile(w["q_norm_g"][0], 2)[:, None], np.tile(w["k_norm_g"][0], 2)[:, None]], axis=1)
    const = np.zeros((P, 5 * P), np.float32)
    const[:, 0:P] = np.eye(P)
    const[:, P:2 * P] = 1.0
    const[:, 2 * P:3 * P] = np.arange(P)
    for m in range(8):
        const[0:64, 3 * P + 16 * m + 2 * m] = 1.0
        const[64:128, 3 * P + 16 * m + 2 * m + 1] = 1.0
    const[:, 4 * P:4 * P + 16] = np.arange(16)
    selt = np.zeros((16, 8 * P), np.float32)
    for m in range(8):
        selt[2 * m, m * P:m * P + 64] = 1.0
        selt[2 * m + 1, m * P + 64:(m + 1) * P] = 1.0
    rel = np.clip(np.arange(P)[:, None] - np.arange(T)[None, :] + 384, -128, 128) + 128
    toep = w["rel_bias"][0][:, rel].transpose(1, 0, 2)
    keys = w["peer_keys"][0].reshape(2 * PH, NKEY, P).transpose(2, 0, 1)
    u = w["peer_u"][0].reshape(NKEY, NKEY, DC, P).transpose(1, 3, 2, 0).reshape(NKEY, P, D)
    v = w["peer_v"][0].reshape(NKEY, GROUPS, 4, 2, 2, 512).transpose(1, 4, 2, 0, 3, 5).reshape(NKEY, P, D)
    return {
        "w_front": f(np.stack(order)), "w_ada": f(units(w["w_ada"][0])), "par": f(par), "const": const,
        "selt": selt, "x": f(w["x"][0].T.reshape(DC, P, T)), "toep": f(toep), "keys": f(keys), "u": f(u), "v": f(v),
    }


def kernel(**inputs):
    import concourse.bacc as bacc
    from concourse.bass_utils import run_bass_kernel_spmd

    arrays = layouts(inputs)
    nc = bacc.Bacc("TRN2", target_bir_lowering=False, num_devices=1)
    aps = [nc.dram_tensor(f"{k}_dram", a.shape, F32, kind="ExternalInput").ap() for k, a in arrays.items()]
    g_d = nc.dram_tensor("g_scratch", (T // TB, P, NKEY * TB), F32, kind="Internal").ap()
    out_d = nc.dram_tensor("out_dram", (DC, P, T), F32, kind="ExternalOutput").ap()
    block_program(nc, *aps, g_d, out_d)
    r = run_bass_kernel_spmd(nc, [{f"{k}_dram": a for k, a in arrays.items()}], core_ids=[0])
    return np.ascontiguousarray(r.results[0]["out_dram"].reshape(1, D, T).transpose(0, 2, 1))
```

```python
from contextlib import ExitStack

import numpy as np

import concourse.bass as bass
from concourse import mybir

ACT = mybir.ActivationFunctionType
ALU = mybir.AluOpType
AX = mybir.AxisListType
F32 = mybir.dt.float32
F32R = mybir.dt.float32r
U32 = mybir.dt.uint32

P = 128
T = 512
D = 1024
DC = D // P
TT = T // P
EPS = 1e-6
HEADS = 8
HD = 64
CHUNK = 64
TAPS = 31
CC = 4
PH = 8
TOPK = 16
NKEY = 128
LOWEST = -3.0e38
MASKED = -1e30
RING = 4

COL = {}
_at = 0
for _name, _n in (("b_ada", 6 * DC), ("g1", DC), ("g2", DC), ("dw", CC * TAPS), ("conv_b", CC),
                  ("ln_g", CC), ("ln_b", CC), ("qg", 1), ("kg", 1)):
    COL[_name] = (_at, _n)
    _at += _n
PAR_COLS = _at

GLU0, QK0, V0, MIX0 = 0, 8, 16, 20
MIX = []
for _m in range(DC):
    MIX += [("gate", _m, 0), ("gate", _m, 1)]
    if _m == 1:
        MIX += [("out", 0), ("out", 1)]
    if _m > 1:
        MIX += [("out", _m)]
WOUT0 = MIX0 + len(MIX)
WQ0 = WOUT0 + DC
FRONT = WQ0 + 2 * PH
SLABS = NKEY
VBASE = FRONT + SLABS
UNITS = VBASE + SLABS
TB = 32
SC = 5
LAG = 3
TOPK_UNITS = 20
MAP_UNITS = 4 * TT
G_FIRST = 40
G_UNITS = 8
G_TURNS = T // (2 * TB)
G_LAST = G_FIRST + G_TURNS * G_UNITS
assert TOPK_UNITS + MAP_UNITS < G_FIRST and G_LAST < SLABS
C_RING = 8
C_LEAD = 3
ADA = 6 * DC
ADA_FIRST = 2 * DC


def block_program(nc, w_front, w_ada, c_d, par_d, const_d, selt_d, x_d, toep_d, keys_d, u_d, v_d, g_d, a_d, out_d):
    ctx = ExitStack()
    with ctx:
        def sb(name, shape, dt=F32):
            return ctx.enter_context(nc.sbuf_tensor("sb_" + name, shape, dt))

        def sem(name):
            return ctx.enter_context(nc.semaphore(name))

        w_hi = sb("w_hi", [P, RING, 1024], F32R)
        w_lo = sb("w_lo", [P, RING, 1024], F32R)
        act_hi = sb("act_hi", [P, DC, T], F32R)
        act_lo = sb("act_lo", [P, DC, T], F32R)
        mix_hi = sb("mix_hi", [P, DC, T], F32R)
        mix_lo = sb("mix_lo", [P, DC, T], F32R)
        stage = sb("stage", [P, RING, 1024])
        x = sb("x", [P, DC, T])
        wide = sb("wide", [P, DC, T])
        par = sb("par", [P, PAR_COLS])
        const = sb("const", [P, 5 * P])
        selt = sb("selt", [16, 8 * P])
        mod = sb("mod", [P, ADA])
        small = sb("small", [P, 160])
        scr = sb("scr", [P, 13952])

        ident = const[:, 0:P]
        ones = const[:, P:2 * P]
        iota = const[:, 2 * P:3 * P]
        sel = const[:, 3 * P:4 * P].rearrange("p (m c) -> p m c", c=16)
        iota16 = const[:, 4 * P:4 * P + 16]

        def col(name, i=0, n=1):
            return par[:, COL[name][0] + i:COL[name][0] + i + n]

        def at(off, shape):
            n = int(np.prod(shape))
            v = scr[:, off:off + n]
            if len(shape) == 2:
                return v.rearrange("p (a b) -> p a b", b=shape[1])
            if len(shape) == 3:
                return v.rearrange("p (a b c) -> p a b c", b=shape[1], c=shape[2])
            return v

        vtok = at(0, [TT, 512])
        y = at(2048, [CC, T])
        U_W = TAPS - 1 + T
        u = at(4096, [CC, U_W])
        toep = at(6272, [2, T])
        r1 = 7296
        ada = at(r1, [4, 1024])
        cond = at(0, [1024])
        ada2 = at(0, [2, 1024])
        cond2 = at(6272, [1024])
        pt = at(r1, [2, TT, T])
        gate = at(r1, [4, T])
        sq = at(11392, [2, T])
        rstd = at(12416, [T])
        sc = at(11392, [SC, T])
        tmp = at(12928, [2, T])
        scores = at(0, [TT, 2 * PH, NKEY])
        keys = at(8192, [2 * PH, NKEY])
        qf = at(10240, [2, T])
        IJW = 3
        wf = wide[:, :, :].rearrange("p a b -> p (a b)")

        def wat(off, n):
            return wf[:, off:off + n]

        sv = wat(0, 1024).rearrange("p (t c k) -> p t c k", t=TT, c=16)
        si = wat(1024, 1024).bitcast(U32).rearrange("p (t c k) -> p t c k", t=TT, c=16)
        top = wat(2048, 512).rearrange("p (t h k) -> p t h k", t=TT, h=PH)
        pos = wat(2560, 512).bitcast(U32).rearrange("p (t h k) -> p t h k", t=TT, h=PH)
        ijw = wat(3072, 3 * P).rearrange("p (c k) -> p c k", c=3)
        rank = wat(3456, 2 * P).rearrange("p (c k) -> p c k", c=2)
        ranku = wat(3712, 2 * P).bitcast(U32).rearrange("p (c k) -> p c k", c=2)
        sif = at(12928, [256])
        hot16 = scr[:, 8192:8192 + 2048]
        mr = at(12928, [2, NKEY])
        cand = at(13184, [256])
        cand2 = at(13440, [256])
        gb = at(0, [2, NKEY, TB])
        hot = scr[:, 8192:8192 + 2048].rearrange("p (s a b) -> p s a b", s=8, a=2)
        ijt = at(10240, [3, T])
        ga = at(11776, [2, T])
        gtile = scr[:, 0:4096].rearrange("p (s b j t) -> p s b j t", s=2, b=T // TB, j=4)
        atile = at(4096, [2, 4, T])
        cf = at(8192, [2, T])
        fin = at(9216, [2, T])

        bank = [ctx.enter_context(nc.psum_tensor(f"bank{b}", [P, 512], F32)) for b in range(8)]
        SB = bank[0:4]
        STAT, XB = bank[1], (bank[2], bank[3])
        UB = bank[4:8]

        par_in = sem("par_in")
        x_in = sem("x_in")
        selt_in = sem("selt_in")
        ada_in = [sem(f"ada_in{i}") for i in range(4)]
        ada2_in = [sem(f"ada2_in{i}") for i in range(2)]
        cond_in = sem("cond_in")
        w_in = [sem(f"w_in{i}") for i in range(RING)]
        toep_in = [sem(f"toep_in{i}") for i in range(2)]
        keys_in = sem("keys_in")
        gt_in = [sem(f"gt_in{i}") for i in range(2)]
        at_in = [sem(f"at_in{i}") for i in range(2)]
        a_out = [sem(f"a_out{i}") for i in range(2)]
        gw_out = [sem(f"gw_out{i}") for i in range(2)]
        out_in = [sem(f"out_in{i}") for i in range(2)]
        w_round = sem("w_round")
        w_split = sem("w_split")
        w_used = sem("w_used")
        cond_ok = sem("cond_ok")
        ada_used = sem("ada_used")
        mod_ok = sem("mod_ok")
        sq_ok = sem("sq_ok")
        sq_used = sem("sq_used")
        ms_ok = sem("ms_ok")
        rt_ok = sem("rt_ok")
        a_pre = sem("a_pre")
        a_hi = sem("a_hi")
        a_lo = sem("a_lo")
        step = sem("step")
        tap_ok = sem("tap_ok")
        sig_ok = sem("sig_ok")
        u_ok = sem("u_ok")
        qk_ok = sem("qk_ok")
        rb_ok = sem("rb_ok")
        qkn_ok = sem("qkn_ok")
        v_sum = sem("v_sum")
        v_ok = sem("v_ok")
        msk_ok = sem("msk_ok")
        s_ok = sem("s_ok")
        sb_ok = sem("sb_ok")
        e_ok = sem("e_ok")
        ri_ok = sem("ri_ok")
        p_ok = sem("p_ok")
        t_ok = sem("t_ok")
        pt_ok = sem("pt_ok")
        o_ok = sem("o_ok")
        conv_ok = sem("conv_ok")
        y_sum = sem("y_sum")
        y_ok = sem("y_ok")
        y_act = sem("y_act")
        y_nrm = sem("y_nrm")
        m_ok = sem("m_ok")
        x2_ok = sem("x2_ok")
        qf_ok = sem("qf_ok")
        ks_ok = sem("ks_ok")
        sc_ok = sem("sc_ok")
        tk_ok = sem("tk_ok")
        te_ok = sem("te_ok")
        ijw_ok = sem("ijw_ok")
        ijt_ok = sem("ijt_ok")
        ijt_cp = sem("ijt_cp")
        hot_ok = sem("hot_ok")
        g_ok = sem("g_ok")
        g_cp = sem("g_cp")
        ge_ok = sem("ge_ok")
        c_mul = sem("c_mul")
        c_hi = sem("c_hi")
        c_lo = sem("c_lo")
        o_part = sem("o_part")
        fin_ok = sem("fin_ok")

        def sums_read(n):
            if n < QK0:
                return (sig_ok if n % 2 == 0 else u_ok), n // 2 + 1
            if n < V0:
                return sq_ok, DC + n - QK0 + 1
            if n < MIX0:
                return v_ok, n - V0 + 1
            if n < WOUT0:
                kind = MIX[n - MIX0]
                return (m_ok, kind[1] + 1) if kind[0] == "out" else (sig_ok, CC + 2 * kind[1] + kind[2] + 1)
            return (x2_ok, n - WOUT0 + 1) if n < WQ0 else (qf_ok, n - WQ0 + 1)

        block = ctx.enter_context(nc.Block())

        @block.sync
        def _(sp):
            sp.dma_start(x[:, :, :], x_d.rearrange("c p t -> p c t")).then_inc(x_in, 16)

            def load(n, src):
                if not isinstance(n, int) or n >= RING:
                    sp.wait_ge(w_split, n - RING + 1)
                return sp.dma_start(stage[:, slot, :], src.rearrange("a p n -> p (a n)"))

            def load_ada(n, k):
                if not isinstance(n, int) or n >= 4:
                    sp.wait_ge(ada_used, n - 3)
                src = w_ada[n:n + 1] if isinstance(n, int) else w_ada[bass.ds(n, 1)]
                sp.dma_start(ada[:, k, :], src.rearrange("a p n -> p (a n)")).then_inc(ada_in[k], 16)

            for n in range(4):
                load_ada(n, n)
            with sp.Fori(1, 3) as turn:
                for k in range(4):
                    load_ada(turn * 4 + k, k)
            for n in range(RING):
                slot = n
                load(n, w_front[n:n + 1]).then_inc(w_in[slot], 16)
            for n in range(12, ADA_FIRST):
                load_ada(n, n % 4)
            with sp.Fori(1, FRONT // RING) as turn:
                for slot in range(RING):
                    load(turn * RING + slot, w_front[bass.ds(turn * RING + slot, 1)]).then_inc(w_in[slot], 16)
            for src_d, base in ((u_d, FRONT), (v_d, VBASE)):
                with sp.Fori(0, SLABS // RING) as turn:
                    for slot in range(RING):
                        load(turn * RING + (base + slot), src_d[bass.ds(turn * RING + slot, 1)]).then_inc(w_in[slot], 16)
            for m in range(DC):
                sp.wait_ge(fin_ok, m + 1)
                sp.dma_start(out_d[m], fin[:, m % 2, :]).then_inc(out_in[m % 2], 16)
            for i in range(2):
                sp.wait_ge(out_in[i], 16 * DC // 2)

        @block.gpsimd
        def _(pool):
            nc.gpsimd.memset(u[:, :, 0:TAPS - 1], 0.0).then_inc(msk_ok, 1)
            for h in range(HEADS):
                if h >= 2:
                    pool.wait_ge(sb_ok, TT * (h - 1))
                pool.dma_start(toep[:, h % 2, :], toep_d[:, h, :]).then_inc(toep_in[h % 2], 16)
                pool.wait_ge(toep_in[h % 2], 16 * (h // 2 + 1))
                nc.gpsimd.memset(toep[0:CHUNK, h % 2, T - CHUNK:T], MASKED).then_inc(msk_ok, 1)
            pool.wait_ge(o_ok, HEADS)
            for n in range(ADA_FIRST, ADA):
                if n >= ADA_FIRST + 2:
                    pool.wait_ge(ada_used, n - 1)
                pool.dma_start(ada2[:, n % 2, :], w_ada[n]).then_inc(ada2_in[n % 2], 16)
            pool.wait_ge(m_ok, DC)
            pool.dma_start(keys[:, :, :], keys_d).then_inc(keys_in, 16)
            with pool.Fori(0, T // TB // 2) as it:
                for s in range(2):
                    pool.wait_ge(g_cp, (it * 2 + (s + 1)) * (TB // 4))
                    pool.dma_start(g_d[bass.ds(it * 2 + s, 1)].rearrange("a p n -> p (a n)"),
                                   gb[:, s, :, :].rearrange("p j t -> p (j t)")).then_inc(gw_out[s], 16)
            for s in range(2):
                pool.wait_ge(gw_out[s], 16 * (T // TB // 2))

            def slab_load(k, s):
                for i in range(2):
                    pool.wait_ge(a_out[i], k * 32 + 32)
                pool.dma_start(gtile[:, s, :, :, :].rearrange("p b j t -> p b (j t)"),
                               g_d[:, :, bass.ds(k * 4 * TB, 4 * TB)].rearrange("b p n -> p b n")
                               ).then_inc(gt_in[s], 16)
                pool.dma_start(atile[:, s, :, :], a_d[bass.ds(k * 4, 4)].rearrange("a p t -> p a t")
                               ).then_inc(at_in[s], 16)

            slab_load(0, 0)
            slab_load(1, 1)
            with pool.Fori(1, SLABS // 8) as kk:
                for s in range(2):
                    pool.wait_ge(c_mul, kk * 8 + (4 * s - 4))
                    slab_load(kk * 2 + s, s)

        def round_unit(act, n, slot):
            act.wait_ge(w_in[slot], 16 * (n // RING + 1) if isinstance(n, int) else n[1])
            nn = n if isinstance(n, int) else n[0]
            if not isinstance(n, int) or n >= RING:
                act.wait_ge(w_used, nn - RING + 1)
            nc.scalar.activation(w_hi[:, slot, :], stage[:, slot, :], ACT.Copy).then_inc(w_round, 1)

        @block.scalar
        def _(act):
            act.dma_start(par[:, :], par_d).then_inc(par_in, 16)
            act.dma_start(const[:, :], const_d).then_inc(par_in, 16)
            act.dma_start(selt[:, :], selt_d).then_inc(selt_in, 16)
            act.dma_start(cond, c_d.to_broadcast([P, D])).then_inc(cond_in, 16)
            act.wait_ge(cond_in, 16)
            nc.scalar.activation(cond, cond, ACT.Silu).then_inc(cond_ok, 1)
            act.wait_ge(x_in, 16)
            squares = 0

            def square(src, used):
                nonlocal squares
                if used > 0:
                    act.wait_ge(sq_used, used)
                nc.scalar.activation(sq[:, squares % 2, :], src, ACT.Square).then_inc(sq_ok, 1)
                squares += 1

            for m in range(DC):
                square(x[:, m, :], squares - 1)
            act.wait_ge(ms_ok, 1)
            nc.scalar.activation(rstd, rstd, ACT.Sqrt).then_inc(rt_ok, 1)
            for n in range(3):
                round_unit(act, n, n % RING)
            hi = 0

            def act_round(m, done):
                nonlocal hi
                act.wait_ge(a_pre, done + m + 1)
                nc.scalar.activation(act_hi[:, m, :], tmp[:, m % 2, :], ACT.Copy).then_inc(a_hi, 1)
                hi += 1

            for m in range(DC):
                act_round(m, 0)

            def evac(n):
                pb = UB[n % 4][:, :]
                act.wait_ge(w_used, n + 1)
                if n < QK0:
                    if n % 2 == 0:
                        i = n // 2
                        if i >= 2:
                            act.wait_ge(u_ok, i - 1)
                        nc.scalar.activation(tmp[:, i % 2, :], pb, ACT.Sigmoid).then_inc(sig_ok, 1)
                elif n < V0:
                    nc.scalar.activation(wide[:, n - QK0, :], pb, ACT.Copy).then_inc(qk_ok, 1)
                    square(pb, squares - 1)
            for n in range(V0 + 1):
                if n >= 1:
                    evac(n - 1)
                round_unit(act, n + 3, (n + 3) % RING)
            act.wait_ge(ms_ok, 2)
            nc.scalar.activation(rstd[0:16, :], rstd[0:16, :], ACT.Sqrt).then_inc(rt_ok, 1)
            for tt in range(TT):
                if tt < TT - 1:
                    act.wait_ge(v_sum, tt + 1)
                else:
                    act.wait_ge(w_used, MIX0)
                nc.scalar.activation(vtok[:, tt, :], UB[tt][:, :], ACT.Copy).then_inc(v_ok, 1)
            for n in range(MIX0, MIX0 + 3):
                round_unit(act, n, n % RING)

            for s in range(HEADS * TT + LAG + 1):
                if s < HEADS * TT:
                    n = (s % TT + 1) * P
                    act.wait_ge(sb_ok, s + 1)
                    nc.scalar.activation(sc[:, s % SC, 0:n], sc[:, s % SC, 0:n], ACT.Exp,
                                         bias=small[:, 120 + s % 8:121 + s % 8],
                                         accum_out=small[:, 128 + s % 8:129 + s % 8]).then_inc(e_ok, 1)
                r = s - 1
                if 0 <= r < HEADS * TT:
                    n = (r % TT + 1) * P
                    act.wait_ge(ri_ok, r + 1)
                    nc.scalar.activation(sc[:, r % SC, 0:n], sc[:, r % SC, 0:n], ACT.Copy,
                                         scale=small[:, 136 + r % 8:137 + r % 8]).then_inc(p_ok, 1)
                r = s - LAG
                if 0 <= r < HEADS * TT:
                    h, q = divmod(r, TT)
                    if h >= 2:
                        act.wait_ge(o_ok, h - 1)
                    act.wait_ge(t_ok, r + 1)
                    n = (q + 1) * P
                    nc.scalar.activation(pt[:, h % 2, 0:q + 1, q * P:(q + 1) * P],
                                         UB[r % 2][:, 0:n].rearrange("p (b q) -> p b q", q=P),
                                         ACT.Copy).then_inc(pt_ok, 1)
                if r in (2 * TT, 4 * TT, 6 * TT):
                    pair = r // (2 * TT) - 1
                    act.wait_ge(o_ok, 2 * pair + 2)
                    nc.scalar.activation(mix_hi[:, CC + pair, :], UB[2 + pair % 2][:, :], ACT.Copy).then_inc(a_hi, 1)
                    hi += 1
            act.wait_ge(o_ok, HEADS)
            nc.scalar.activation(mix_hi[:, CC + 3, :], UB[3][:, :], ACT.Copy).then_inc(a_hi, 1)
            hi += 1

            act.dma_start(cond2, c_d.to_broadcast([P, D])).then_inc(cond_in, 16)
            act.wait_ge(cond_in, 32)
            nc.scalar.activation(cond2, cond2, ACT.Silu).then_inc(cond_ok, 1)

            def mix_evac(n):
                kind = MIX[n - MIX0]
                if kind[0] == "gate":
                    _, m, br = kind
                    act.wait_ge(w_used, n + 1)
                    if m >= 2:
                        act.wait_ge(m_ok, m - 1)
                    nc.scalar.activation(gate[:, 2 * (m % 2) + br, :], UB[n % 4][:, :], ACT.Sigmoid).then_inc(sig_ok, 1)

            for n in range(MIX0, WOUT0):
                if n > MIX0:
                    mix_evac(n - 1)
                round_unit(act, n + 3, (n + 3) % RING)
                if n == MIX0 + 1:
                    for i in range(CC):
                        act.wait_ge(y_ok, i + 1)
                        square(y[:, i, :], squares - 1)
                    act.wait_ge(ms_ok, 4)
                    nc.scalar.activation(rstd, rstd, ACT.Sqrt).then_inc(rt_ok, 1)
                if n == MIX0 + 3:
                    for i in range(CC):
                        act.wait_ge(y_nrm, i + 1)
                        nc.scalar.activation(y[:, i, :], y[:, i, :], ACT.Silu, scale=col("ln_g", i),
                                             bias=col("ln_b", i)).then_inc(y_act, 1)
                        act.wait_ge(y_act, i + 1)
                        nc.scalar.activation(mix_hi[:, i, :], y[:, i, :], ACT.Copy).then_inc(a_hi, 1)
                        hi += 1

            def merged_round(m):
                nonlocal hi
                if m == 0:
                    act.wait_ge(w_used, WOUT0 - 1)
                act.wait_ge(m_ok, m + 1)
                nc.scalar.activation(act_hi[:, m, :], wide[:, m, :], ACT.Copy).then_inc(a_hi, 1)
                hi += 1

            for m in range(DC):
                merged_round(m)
            for n in range(WOUT0, WQ0):
                m = n - WOUT0 - 1
                if m >= 0:
                    act.wait_ge(x2_ok, m + 1)
                    square(x[:, m, :], squares - 1)
                round_unit(act, n + 3, (n + 3) % RING)
            act.wait_ge(x2_ok, DC)
            square(x[:, DC - 1, :], squares - 1)
            act.wait_ge(ms_ok, 5)
            nc.scalar.activation(rstd, rstd, ACT.Sqrt).then_inc(rt_ok, 1)
            for m in range(DC):
                act_round(m, DC)

            def wq_evac(c):
                n = WQ0 + c
                act.wait_ge(w_used, n + 1)
                if c >= 2:
                    act.wait_ge(ks_ok, c - 1)
                nc.scalar.activation(qf[:, c % 2, :], UB[n % 4][:, :], ACT.Copy).then_inc(qf_ok, 1)

            def ks_evac(c):
                act.wait_ge(ks_ok, c + 1)
                nc.scalar.activation(scores[:, :, c, :], XB[c % 2][:, :].rearrange("p (t k) -> p t k", t=TT),
                                     ACT.Copy).then_inc(sc_ok, 1)

            for c in range(2 * PH):
                if c >= 1:
                    wq_evac(c - 1)
                round_unit(act, WQ0 + c + 3, (WQ0 + c + 3) % RING)
                if c >= 2:
                    ks_evac(c - 2)
            wq_evac(2 * PH - 1)
            ks_evac(2 * PH - 2)
            ks_evac(2 * PH - 1)
            def slab(t, per, b, first=False):
                q = t * per + b
                if not first:
                    k = (b - 1) % 4
                    act.wait_ge(w_used, q + FRONT)
                    if not isinstance(q, int) or q >= 3:
                        act.wait_ge(a_out[k % 2], (t * (per // 2) + (b - 1) // 2) * 16)
                    nc.scalar.activation(ga[:, k % 2, :], UB[k][:, :], ACT.Gelu).then_inc(ge_ok, 1)
                turns = t * (per // 4) + (FRONT // RING + 1 + (b + 3) // 4)
                round_unit(act, (q + (FRONT + 3), turns * 16), (b + 3) % RING)
                if not first:
                    act.wait_ge(ge_ok, q)
                    src, dst = ga[:, k % 2, :], a_d[bass.ds(q - 1, 1)].rearrange("a p t -> p (a t)")
                    act.dma_start(dst, src).then_inc(a_out[k % 2], 16)

            for q in range(TOPK_UNITS):
                slab(0, 4, q, q == 0)
            for q in range(TOPK_UNITS, G_FIRST):
                slab(0, 4, q)
                if q == TOPK_UNITS + 1:
                    for tt in range(TT):
                        act.wait_ge(tk_ok, tt + 1)
                        v = top[:, tt, :, :].rearrange("p h k -> p (h k)")
                        nc.scalar.activation(v, v, ACT.Exp).then_inc(te_ok, 1)
                tt, at_unit = divmod(q - TOPK_UNITS - 5, 4)
                if at_unit == 0 and 0 <= tt < TT:
                    act.wait_ge(ijt_ok, tt + 1)
                    nc.scalar.activation(ijt[:, :, tt * P:(tt + 1) * P], XB[tt % 2][:, 0:3 * P].rearrange(
                        "p (c t) -> p c t", c=3), ACT.Copy).then_inc(ijt_cp, 1)

            def g_turn(it, first):
                for b in range(G_UNITS):
                    slab(it, G_UNITS, G_FIRST + b)
                    for j in (2 * b, 2 * b + 1):
                        s, o = divmod(4 * j, TB)
                        if o == 0 and not first:
                            act.wait_ge(gw_out[s], it * 16)
                        act.wait_ge(g_ok, it * (2 * TB // 4) + (j + 1))
                        nc.scalar.activation(gb[:, s, :, o:o + 4].rearrange("p j t -> p t j"),
                                             bank[j % 4][:, :].rearrange("p (t j) -> p t j", t=4),
                                             ACT.Copy).then_inc(g_cp, 1)

            g_turn(0, True)
            with act.Fori(1, G_TURNS) as it:
                g_turn(it, False)
            with act.Fori(G_LAST // 4, SLABS // 4 - 1) as turn:
                for b in range(4):
                    slab(turn, 4, b)

            def coefficients(r, b):
                act.wait_ge(c_mul, r + 1)
                act.wait_ge(w_used, r + (VBASE - C_RING + 1))
                nc.scalar.activation(mix_hi[:, b % C_RING, :], cf[:, b % 2, :], ACT.Copy).then_inc(c_hi, 1)

            for b in range(4):
                slab(SLABS // 4 - 1, 4, b)
                if b:
                    coefficients(b - 1, b - 1)

            def v_turn(t, last):
                for b in range(C_RING):
                    r = t * C_RING + b
                    if isinstance(t, int) and r == 0:
                        slab_end()
                    if not (last and b + 3 >= C_RING):
                        turns = t * 2 + (VBASE // RING + 1 + (b + 3) // 4)
                        round_unit(act, (r + (VBASE + 3), turns * 16), (b + 3) % RING)
                    if not (last and b + C_LEAD >= C_RING):
                        coefficients(r + C_LEAD, b + C_LEAD)

            def slab_end():
                act.wait_ge(w_used, VBASE)
                act.wait_ge(a_out[1], 16 * (SLABS // 2 - 1))
                nc.scalar.activation(ga[:, 1, :], UB[3][:, :], ACT.Gelu).then_inc(ge_ok, 1)
                act.wait_ge(ge_ok, SLABS)
                act.dma_start(a_d[SLABS - 1], ga[:, 1, :]).then_inc(a_out[1], 16)

            v_turn(0, False)
            with act.Fori(1, SLABS // C_RING - 1) as t:
                v_turn(t, False)
            v_turn(SLABS // C_RING - 1, True)

        @block.vector
        def _(dve):
            count = {"step": 0}

            def link(ins):
                count["step"] += 1
                ins.then_inc(step, 1)
                dve.wait_ge(step, count["step"])

            def mark(ins):
                count["step"] += 1
                ins.then_inc(step, 1)
                return count["step"]

            def split_unit(n, slot):
                dve.wait_ge(w_round, n + 1)
                nc.vector.tensor_tensor(w_lo[:, slot, :], stage[:, slot, :], w_hi[:, slot, :].bitcast(F32),
                                        ALU.subtract).then_inc(w_split, 1)

            lo = 0

            def lo_part(dst, src, hi_ap):
                nonlocal lo
                dve.wait_ge(a_hi, lo + 1)
                nc.vector.tensor_tensor(dst, src, hi_ap.bitcast(F32), ALU.subtract).then_inc(a_lo, 1)
                lo += 1

            def ada_unit(n, src, by, arrived, value):
                dve.wait_ge(arrived, value)
                nc.vector.tensor_tensor_reduce(src, src, by, 1.0, 0.0, ALU.mult, ALU.add,
                                               mod[:, n:n + 1]).then_inc(ada_used, 1)

            def ada_rest(n):
                if n == ADA_FIRST:
                    dve.wait_ge(cond_ok, 2)
                ada_unit(n, ada2[:, n % 2, :], cond2, ada2_in[n % 2], 16 * ((n - ADA_FIRST) // 2 + 1))

            dve.wait_ge(par_in, 32)
            link(nc.vector.tensor_scalar(small[:, 40:41], col("qg"), HD ** -0.5, None, ALU.mult))

            def norm_scale(width):
                count["ms"] = count.get("ms", 0) + 1
                nc.vector.tensor_scalar(rstd, STAT[:, :], 1.0 / width, EPS, ALU.mult, ALU.add).then_inc(ms_ok, 1)
                dve.wait_ge(rt_ok, count["ms"])
                link(nc.vector.reciprocal(rstd, rstd))

            def modulated(a0, b0, w_first):
                for m in range(DC + 1):
                    if m < DC:
                        if m >= 2:
                            dve.wait_ge(a_lo, lo)
                        link(nc.vector.tensor_tensor(tmp[:, m % 2, :], x[:, m, :], rstd, ALU.mult))
                        nc.vector.tensor_scalar(tmp[:, m % 2, :], tmp[:, m % 2, :], small[:, a0 + m:a0 + m + 1],
                                                mod[:, b0 + m:b0 + m + 1], ALU.mult, ALU.add).then_inc(a_pre, 1)
                    if m >= 1:
                        lo_part(act_lo[:, m - 1, :], tmp[:, (m - 1) % 2, :], act_hi[:, m - 1, :])
                    if m in (3, 5) and w_first is not None:
                        split_unit(w_first + (m - 3) // 2, (w_first + (m - 3) // 2) % RING)

            dve.wait_ge(cond_ok, 1)
            for n in range(ADA_FIRST - 4):
                ada_unit(n, ada[:, n % 4, :], cond, ada_in[n % 4], 16 * (n // 4 + 1))
            dve.wait_ge(sq_used, DC)
            norm_scale(D)
            for n in range(ADA_FIRST - 4, ADA_FIRST):
                ada_unit(n, ada[:, n % 4, :], cond, ada_in[n % 4], 16 * (n // 4 + 1))
            dve.wait_ge(ada_used, ADA_FIRST)
            link(nc.vector.tensor_tensor(mod[:, 0:ADA_FIRST], mod[:, 0:ADA_FIRST], col("b_ada", 0, ADA_FIRST), ALU.add))
            link(nc.vector.tensor_scalar(small[:, 8:16], mod[:, DC:2 * DC], 1.0, None, ALU.add))
            link(nc.vector.tensor_tensor(small[:, 8:16], small[:, 8:16], col("g1", 0, DC), ALU.mult))
            modulated(8, 0, 0)

            def conv(first, n):
                for k in range(first, min(first + n, CC * TAPS)):
                    pair, k2 = divmod(k, 2 * TAPS)
                    w, i = k2 // 2, 2 * pair + k2 % 2
                    src, wt = u[:, i, w:w + T], col("dw", i * TAPS + w)
                    if w == 0:
                        dve.wait_ge(u_ok, i + 1)
                        dve.wait_ge(msk_ok, 1)
                        ins = nc.vector.tensor_scalar(y[:, i, :], src, wt, col("conv_b", i), ALU.mult, ALU.add)
                    else:
                        dve.wait_ge(tap_ok, k - 1)
                        ins = nc.vector.scalar_tensor_tensor(out=y[:, i, :], in0=src, scalar=wt, in1=y[:, i, :],
                                                             op0=ALU.mult, op1=ALU.add)
                    ins.then_inc(tap_ok, 1)
                return first + n

            done = 0

            for n in range(MIX0):
                if n <= V0:
                    split_unit(n + 2, (n + 2) % RING)
                if n == V0:
                    split_unit(n + 3, (n + 3) % RING)
                j = n - 1
                if 0 <= j < QK0 and j % 2 == 1:
                    i = j // 2
                    dve.wait_ge(w_used, j + 1)
                    dve.wait_ge(sig_ok, i + 1)
                    nc.vector.tensor_tensor(u[:, i, TAPS - 1:], tmp[:, i % 2, :], UB[j % 4][:, :],
                                            ALU.mult).then_inc(u_ok, 1)
                if n == V0:
                    dve.wait_ge(sq_used, 2 * DC)
                    count["ms"] += 1
                    nc.vector.tensor_scalar(rstd[0:16, :], STAT[0:16, :], 1.0 / HD, EPS, ALU.mult, ALU.add
                                            ).then_inc(ms_ok, 1)
                    dve.wait_ge(rt_ok, 2)
                    nc.vector.reciprocal(rstd[0:16, :], rstd[0:16, :]).then_inc(ms_ok, 1)
                if n > V0:
                    for m in range((n - V0 - 1) * 3, min((n - V0) * 3, 8)):
                        dve.wait_ge(rb_ok, m + 1)
                        dve.wait_ge(qk_ok, m + 1)
                        nc.vector.scalar_tensor_tensor(out=wide[:, m, :], in0=wide[:, m, :],
                                                       scalar=small[:, 40:41] if m < 4 else col("kg"),
                                                       in1=XB[m % 2][:, :], op0=ALU.mult, op1=ALU.mult
                                                       ).then_inc(qkn_ok, 1)
                if n >= 4:
                    done = conv(done, 6 if n < V0 else 5)

            for n in range(MIX0, MIX0 + 3):
                split_unit(n, n % RING)

            def o_lo(pair):
                nonlocal lo
                dve.wait_ge(a_hi, lo + 1)
                nc.vector.tensor_tensor(mix_lo[:, CC + pair, :], UB[2 + pair % 2][:, :],
                                        mix_hi[:, CC + pair, :].bitcast(F32), ALU.subtract).then_inc(a_lo, 1)
                lo += 1

            for s in range(HEADS * TT + 1):
                if s < HEADS * TT:
                    h, q = divmod(s, TT)
                    n = (q + 1) * P
                    if s >= SC:
                        dve.wait_ge(t_ok, s - SC + 1)
                    dve.wait_ge(s_ok, s + 1)
                    dve.wait_ge(msk_ok, h + 2)
                    link(nc.vector.tensor_tensor_reduce(sc[:, s % SC, 0:n], SB[s % 4][:, 0:n],
                                                        toep[:, h % 2, T - n:T], 1.0, LOWEST, ALU.add, ALU.max,
                                                        small[:, 112 + s % 8:113 + s % 8]))
                    nc.vector.tensor_scalar(small[:, 120 + s % 8:121 + s % 8], small[:, 112 + s % 8:113 + s % 8], -1.0,
                                            None, ALU.mult).then_inc(sb_ok, 1)
                r = s - 1
                if r >= 0:
                    n = (r % TT + 1) * P
                    dve.wait_ge(e_ok, r + 1)
                    nc.vector.reciprocal(small[:, 136 + r % 8:137 + r % 8], small[:, 128 + r % 8:129 + r % 8]
                                         ).then_inc(ri_ok, 1)
                done = conv(done, 1)
                if s >= 2 * TT + 4 and (s - 4) % (2 * TT) == 0:
                    o_lo((s - 4) // (2 * TT) - 1)
            conv(done, CC * TAPS)

            def merge(m):
                n = MIX0 + MIX.index(("out", m))
                dve.wait_ge(w_used, n + 1)
                dve.wait_ge(sig_ok, CC + 2 * m + 2)
                a = mark(nc.vector.tensor_tensor(gate[:, 2 * (m % 2), :], gate[:, 2 * (m % 2), :], UB[n % 4][:, :], ALU.mult))
                b = mark(nc.vector.tensor_tensor(gate[:, 2 * (m % 2) + 1, :], gate[:, 2 * (m % 2) + 1, :], XB[m % 2][:, :],
                                                 ALU.mult))
                dve.wait_ge(step, b)
                nc.vector.tensor_tensor(wide[:, m, :], gate[:, 2 * (m % 2), :], gate[:, 2 * (m % 2) + 1, :],
                                        ALU.add).then_inc(m_ok, 1)

            dve.wait_ge(tap_ok, CC * TAPS)
            nc.vector.memset(small[:, 60:61], 0.0).then_inc(conv_ok, 1)
            o_lo(3)
            dve.wait_ge(y_sum, 1)
            link(nc.vector.tensor_scalar(rstd, XB[0][:, :], 1.0 / 512, None, ALU.mult))
            for i in range(CC):
                nc.vector.tensor_tensor(y[:, i, :], y[:, i, :], rstd, ALU.subtract).then_inc(y_ok, 1)
            split_unit(MIX0 + 3, (MIX0 + 3) % RING)
            dve.wait_ge(sq_used, 2 * DC + CC)
            norm_scale(512)
            split_unit(MIX0 + 4, (MIX0 + 4) % RING)
            for i in range(CC):
                nc.vector.tensor_tensor(y[:, i, :], y[:, i, :], rstd, ALU.mult).then_inc(y_nrm, 1)
            for i in range(CC):
                lo_part(mix_lo[:, i, :], y[:, i, :], mix_hi[:, i, :])
            for n in range(3):
                ada_rest(ADA_FIRST + n)
            for n in range(MIX0 + 3, WOUT0):
                split_unit(n + 2, (n + 2) % RING)
                ada_rest(ADA_FIRST + n - MIX0)
                if MIX[n - 1 - MIX0][0] == "out":
                    merge(MIX[n - 1 - MIX0][1])
            for m in range(DC - 1):
                lo_part(act_lo[:, m, :], wide[:, m, :], act_hi[:, m, :])
            merge(DC - 1)
            lo_part(act_lo[:, DC - 1, :], wide[:, DC - 1, :], act_hi[:, DC - 1, :])

            n1 = ADA_FIRST + WOUT0 - MIX0
            dve.wait_ge(ada_used, n1)
            link(nc.vector.tensor_tensor(mod[:, ADA_FIRST:n1], mod[:, ADA_FIRST:n1],
                                         col("b_ada", ADA_FIRST, n1 - ADA_FIRST), ALU.add))
            link(nc.vector.tensor_scalar(small[:, 16:24], mod[:, 4 * DC:5 * DC], 1.0, None, ALU.add))
            link(nc.vector.tensor_tensor(small[:, 16:24], small[:, 16:24], col("g2", 0, DC), ALU.mult))
            for n in range(WOUT0, WQ0 + 1):
                if n < WQ0:
                    split_unit(n + 2, (n + 2) % RING)
                    ada_rest(ADA_FIRST + n - MIX0)
                m = n - 1 - WOUT0
                if m >= 0:
                    dve.wait_ge(w_used, n)
                    nc.vector.scalar_tensor_tensor(out=x[:, m, :], in0=UB[(n - 1) % 4][:, :],
                                                   scalar=mod[:, 2 * DC + m:2 * DC + m + 1], in1=x[:, m, :],
                                                   op0=ALU.mult, op1=ALU.add).then_inc(x2_ok, 1)
            dve.wait_ge(ada_used, ADA)
            link(nc.vector.tensor_tensor(mod[:, n1:ADA], mod[:, n1:ADA], col("b_ada", n1, ADA - n1), ALU.add))
            dve.wait_ge(sq_used, 3 * DC + CC)
            norm_scale(D)
            modulated(16, 3 * DC, None)

            def topk(tt, h):
                if h == 0 and tt == 0:
                    dve.wait_ge(a_lo, lo)
                dve.wait_ge(sc_ok, 2 * h + 2)
                last = {}
                for part in range(5):
                    for p in range(2):
                        s = scores[:, tt, 2 * h + p, :]
                        v, ix = sv[:, tt, 2 * h + p, :], si[:, tt, 2 * h + p, :]
                        if part:
                            dve.wait_ge(step, last[p])
                        if part == 0:
                            ins = nc.vector.max(v[:, 0:8], s)
                        elif part == 1:
                            ins = nc.vector.max_index(ix[:, 0:8], v[:, 0:8], s)
                        elif part == 2:
                            ins = nc.vector.match_replace(mr[:, p, :], v[:, 0:8], s, LOWEST)
                        elif part == 3:
                            ins = nc.vector.max(v[:, 8:16], mr[:, p, :])
                        else:
                            ins = nc.vector.max_index(ix[:, 8:16], v[:, 8:16], mr[:, p, :])
                        last[p] = mark(ins)
                a = sv[:, tt, 2 * h, :].rearrange("p (k o) -> p k o", o=1).to_broadcast([P, TOPK, TOPK])
                b = sv[:, tt, 2 * h + 1, :].rearrange("p (o k) -> p o k", o=1).to_broadcast([P, TOPK, TOPK])
                link(nc.vector.tensor_tensor(cand.rearrange("p (a b) -> p a b", b=TOPK), a, b, ALU.add))
                link(nc.vector.max(top[:, tt, h, 0:8], cand))
                mark(nc.vector.max_index(pos[:, tt, h, 0:8], top[:, tt, h, 0:8], cand))
                link(nc.vector.match_replace(cand2, top[:, tt, h, 0:8], cand, LOWEST))
                link(nc.vector.max(top[:, tt, h, 8:16], cand2))
                link(nc.vector.max_index(pos[:, tt, h, 8:16], top[:, tt, h, 8:16], cand2))

            for c in range(2 * PH):
                split_unit(WQ0 + c + 2, (WQ0 + c + 2) % RING)
                if c >= 4:
                    topk((c - 4) % TT, (c - 4) // TT)
            for q in range(TOPK_UNITS):
                split_unit(FRONT + q + 2, (q + 2) % RING)
                job = 2 * PH - 4 + q
                topk(job % TT, job // TT)
            link(nc.vector.tensor_copy(small[:, 80:112].rearrange("p (t h) -> p t h", t=TT), top[:, :, :, 0]))
            for tt in range(TT):
                nc.vector.tensor_tensor(top[:, tt, :, :], top[:, tt, :, :],
                                        small[:, 80 + PH * tt:80 + PH * tt + PH].rearrange(
                                            "p (h o) -> p h o", o=1).to_broadcast([P, PH, TOPK]), ALU.subtract
                                        ).then_inc(tk_ok, 1)
            eq = hot16.rearrange("p (c r) -> p c r", r=TOPK)
            eq4 = hot16.rearrange("p (h k r) -> p h k r", h=PH, k=TOPK)
            def indices(tt, part):
                pv = pos[:, tt, :, :].rearrange("p h k -> p (h k)")
                if part == 0:
                    mark(nc.vector.tensor_scalar(ranku[:, 0, :], pv, 4, None, ALU.logical_shift_right))
                    mark(nc.vector.tensor_scalar(ranku[:, 1, :], pv, 15, None, ALU.bitwise_and))
                    link(nc.vector.tensor_copy(sif, si[:, tt, :, :].rearrange("p c k -> p (c k)")))
                    link(nc.vector.tensor_copy(rank[:, :, :], ranku[:, :, :]))
                    if tt:
                        dve.wait_ge(ijt_ok, tt)
                if part < 2:
                    link(nc.vector.tensor_tensor(eq, rank[:, part, :].rearrange("p (c o) -> p c o", o=1).to_broadcast(
                        [P, P, TOPK]), iota16.rearrange("p (o r) -> p o r", o=1).to_broadcast([P, P, TOPK]),
                        ALU.is_equal))
                if part < 2:
                    six = sif.rearrange("p (h two r) -> p h two r", h=PH, two=2)[:, :, part:part + 1, :]
                    link(nc.vector.tensor_tensor(eq4, eq4, six.to_broadcast([P, PH, TOPK, TOPK]), ALU.mult))
                    link(nc.vector.tensor_reduce(ijw[:, part, :], eq, AX.X, ALU.add))
                if part == 2:
                    dve.wait_ge(te_ok, tt + 1)
                    e = top[:, tt, :, :]
                    link(nc.vector.tensor_reduce(small[:, 64:72], e, AX.X, ALU.add))
                    link(nc.vector.reciprocal(small[:, 72:80], small[:, 64:72]))
                    nc.vector.tensor_tensor(ijw[:, 2, :].rearrange("p (h k) -> p h k", h=PH), e,
                                            small[:, 72:80].rearrange("p (h o) -> p h o", o=1).to_broadcast(
                                                [P, PH, TOPK]), ALU.mult).then_inc(ijw_ok, 1)
                    dve.wait_ge(ijw_ok, tt + 1)

            for q in range(TOPK_UNITS, G_FIRST):
                split_unit(FRONT + q + 2, (q + 2) % RING)
                tt, part = divmod(q - TOPK_UNITS, 4)
                if tt < TT:
                    indices(tt, part)

            dve.wait_ge(ijt_cp, TT)

            def g_turn(it, first):
                for b in range(G_UNITS):
                    split_unit(it * G_UNITS + (FRONT + G_FIRST + b + 2), (b + 2) % RING)
                    for t in range(8 * b, 8 * b + 8):
                        if t % 4 == 0 and not (first and t < 8):
                            dve.wait_ge(g_ok, it * (2 * TB // 4) + (t // 4 - 1))
                        icol, jcol, wcol = (ijt[:, c, bass.ds(it * (2 * TB) + t, 1)] for c in range(3))
                        nc.vector.tensor_scalar(hot[:, t % 8, 0, :], iota, icol, None, ALU.is_equal).then_inc(hot_ok, 1)
                        nc.vector.tensor_scalar(hot[:, t % 8, 1, :], iota, jcol, wcol, ALU.is_equal, ALU.mult
                                                ).then_inc(hot_ok, 1)

            g_turn(0, True)
            with dve.Fori(1, G_TURNS) as it:
                g_turn(it, False)
            with dve.Fori(G_LAST // 4, SLABS // 4 - 1) as turn:
                for b in range(4):
                    split_unit(turn * 4 + (FRONT + b + 2), (b + 2) % RING)

            def multiply(r, t, b):
                s = b // 4 % 2
                if b % 4 == 0:
                    dve.wait_ge(gt_in[s], (t + (b // 8 + 1)) * 16)
                    dve.wait_ge(at_in[s], (t + (b // 8 + 1)) * 16)
                if not isinstance(r, int) or r >= 2:
                    dve.wait_ge(c_lo, r - 1)
                nc.vector.tensor_tensor(cf[:, b % 2, :].rearrange("p (b t) -> p b t", t=TB),
                                        atile[:, s, b % 4, :].rearrange("p (b t) -> p b t", t=TB),
                                        gtile[:, s, :, b % 4, :], ALU.mult).then_inc(c_mul, 1)

            def coef_lo(r, b):
                dve.wait_ge(c_hi, r + 1)
                nc.vector.tensor_tensor(mix_lo[:, b % C_RING, :], cf[:, b % 2, :],
                                        mix_hi[:, b % C_RING, :].bitcast(F32), ALU.subtract).then_inc(c_lo, 1)

            for b in range(4):
                if b:
                    multiply(b - 1, 0, b - 1)
                split_unit(VBASE - 4 + b + 2, (b + 2) % RING)
                if b:
                    coef_lo(b - 1, b - 1)

            def v_turn(t, last):
                for b in range(C_RING):
                    r = t * C_RING + b
                    more = not (last and b + C_LEAD >= C_RING)
                    if more:
                        multiply(r + C_LEAD, t, b + C_LEAD)
                    if not (last and b + 2 >= C_RING):
                        split_unit(r + (VBASE + 2), (b + 2) % RING)
                    if more:
                        coef_lo(r + C_LEAD, b + C_LEAD)

            v_turn(0, False)
            with dve.Fori(1, SLABS // C_RING - 1) as t:
                v_turn(t, False)
            v_turn(SLABS // C_RING - 1, True)

            for m in range(DC):
                if m < DC - 1:
                    dve.wait_ge(o_part, m + 1)
                else:
                    dve.wait_ge(w_used, UNITS)
                if m >= 2:
                    dve.wait_ge(out_in[m % 2], 16 * (m // 2))
                nc.vector.scalar_tensor_tensor(out=fin[:, m % 2, :], in0=bank[m][:, :],
                                               scalar=mod[:, 5 * DC + m:5 * DC + m + 1], in1=x[:, m, :],
                                               op0=ALU.mult, op1=ALU.add).then_inc(fin_ok, 1)

        @block.tensor
        def _(pe):
            sums = 0

            def sum_squares(m, n, lhs=None, out=None):
                nonlocal sums
                pe.wait_ge(sq_ok, sums + 1)
                nc.tensor.matmul(STAT[:, :] if out is None else out, ones if lhs is None else lhs,
                                 sq[:, sums % 2, :], start=(m == 0), stop=(m == n - 1)).then_inc(sq_used, 1)
                sums += 1

            def product(out, slot, dcs, rhs_hi, rhs_lo, col0=0):
                for i, dc in enumerate(dcs):
                    w = slice(col0 + dc * P, col0 + (dc + 1) * P)
                    nc.tensor.matmul(out, w_hi[:, slot, w], rhs_hi[:, dc, :], start=(i == 0), stop=False)
                    nc.tensor.matmul(out, w_hi[:, slot, w], rhs_lo[:, dc, :], start=False, stop=False)
                    last = nc.tensor.matmul(out, w_lo[:, slot, w], rhs_hi[:, dc, :], start=False,
                                            stop=(i == len(dcs) - 1))
                return last

            def unit(n, rhs_hi, rhs_lo, first_lo=None):
                pe.wait_ge(w_split, n + 1)
                if n >= 4:
                    pe.wait_ge(*sums_read(n - 4))
                if first_lo is None:
                    product(UB[n % 4][:, :], n % RING, range(DC), rhs_hi, rhs_lo).then_inc(w_used, 1)
                    return
                for dc in range(DC):
                    pe.wait_ge(a_lo, first_lo + dc + 1)
                    w = slice(dc * P, (dc + 1) * P)
                    nc.tensor.matmul(UB[n % 4][:, :], w_hi[:, n % RING, w], rhs_hi[:, dc, :], start=(dc == 0), stop=False)
                    nc.tensor.matmul(UB[n % 4][:, :], w_hi[:, n % RING, w], rhs_lo[:, dc, :], start=False, stop=False)
                    last = nc.tensor.matmul(UB[n % 4][:, :], w_lo[:, n % RING, w], rhs_hi[:, dc, :], start=False,
                                            stop=(dc == DC - 1))
                last.then_inc(w_used, 1)

            pe.wait_ge(par_in, 32)
            for m in range(DC):
                sum_squares(m, DC)
            for n in range(V0):
                unit(n, act_hi, act_lo, 0 if n == 0 else None)
                if n > QK0:
                    sum_squares(n - 1 - QK0, DC, sel[:, n - 1 - QK0, :], STAT[0:16, :])
            sum_squares(DC - 1, DC, sel[:, DC - 1, :], STAT[0:16, :])
            pe.wait_ge(selt_in, 16)
            pe.wait_ge(w_split, MIX0)
            for tt in range(TT):
                pe.wait_ge(*sums_read(V0 - 4 + tt))
                t = slice(tt * P, (tt + 1) * P)
                for dc in range(DC):
                    w = slice(dc * P, (dc + 1) * P)
                    nc.tensor.matmul(UB[tt][:, :], act_hi[:, dc, t], w_hi[:, :, w], start=(dc == 0), stop=False)
                    nc.tensor.matmul(UB[tt][:, :], act_hi[:, dc, t], w_lo[:, :, w], start=False, stop=False)
                    last = nc.tensor.matmul(UB[tt][:, :], act_lo[:, dc, t], w_hi[:, :, w], start=False,
                                            stop=(dc == DC - 1))
                if tt < TT - 1:
                    last.then_inc(v_sum, 1)
                else:
                    last.then_inc(w_used, RING)
                for m in range(max(0, 3 * tt - 3), min(3 * tt, 8)):
                    if m == 0:
                        pe.wait_ge(ms_ok, 3)
                    if m >= 2:
                        pe.wait_ge(qkn_ok, m - 1)
                    nc.tensor.matmul(XB[m % 2][:, :], selt[:, m * P:(m + 1) * P], rstd[0:16, :],
                                     start=True, stop=True).then_inc(rb_ok, 1)

            pe.wait_ge(qkn_ok, 8)
            pe.wait_ge(v_ok, 4)
            for s in range(HEADS * TT + LAG + 1):
                if s < HEADS * TT:
                    h, q = divmod(s, TT)
                    base = HD * (h % 2)
                    n = (q + 1) * P
                    if s >= 4:
                        pe.wait_ge(sb_ok, s - 3)
                    nc.tensor.matmul(SB[s % 4][:, 0:n], wide[base:base + HD, h // 2, q * P:(q + 1) * P],
                                     wide[base:base + HD, 4 + h // 2, 0:n], start=True, stop=True).then_inc(s_ok, 1)
                r = s - LAG
                if 0 <= r < HEADS * TT:
                    pe.wait_ge(p_ok, r + 1)
                    if r >= 2:
                        pe.wait_ge(pt_ok, r - 1)
                    for b in range(r % TT + 1):
                        last = nc.tensor.transpose(UB[r % 2][:, b * P:(b + 1) * P], sc[:, r % SC, b * P:(b + 1) * P], ident)
                    last.then_inc(t_ok, 1)
                r = s - LAG - 1
                if r >= 0 and r % TT == TT - 1:
                    h = r // TT
                    pair = h // 2
                    if pair >= 2 and h % 2 == 0:
                        pe.wait_ge(a_lo, DC + pair - 1)
                    pe.wait_ge(pt_ok, r + 1)
                    base = HD * (h % 2)
                    for kb in range(TT):
                        last = nc.tensor.matmul(UB[2 + pair % 2][base:base + HD, kb * P:T],
                                                vtok[:, kb, h * HD:(h + 1) * HD], pt[:, h % 2, kb, kb * P:T],
                                                start=(kb == 0), stop=(kb == TT - 1))
                    last.then_inc(o_ok, 1)

            pe.wait_ge(pt_ok, HEADS * TT)
            pe.wait_ge(sb_ok, HEADS * TT)

            def mix_unit(n):
                kind = MIX[n - MIX0]
                if kind[0] == "gate":
                    if n - MIX0 < 4 and n % 4 >= 2:
                        pe.wait_ge(a_lo, DC + CC)
                    unit(n, act_hi, act_lo)
                    return
                m = kind[1]
                pe.wait_ge(w_split, n + 1)
                pe.wait_ge(*sums_read(n - 4))
                if m >= 2:
                    pe.wait_ge(m_ok, m - 1)
                if m == 0:
                    pe.wait_ge(a_lo, DC + 2 * CC)
                product(UB[n % 4][:, :], n % RING, range(CC), mix_hi, mix_lo)
                product(XB[m % 2][:, :], n % RING, range(CC, 2 * CC), mix_hi, mix_lo).then_inc(w_used, 1)

            pe.wait_ge(conv_ok, 1)
            mix_unit(MIX0)
            for i in range(CC):
                last = nc.tensor.matmul(XB[0][:, :], ones, y[:, i, :], start=(i == 0), stop=(i == CC - 1))
            last.then_inc(y_sum, 1)
            mix_unit(MIX0 + 1)
            for i in range(CC):
                sum_squares(i, CC)
            for n in range(MIX0 + 2, WOUT0):
                mix_unit(n)
            merged_lo = DC + 2 * CC
            for n in range(WOUT0, WQ0):
                unit(n, act_hi, act_lo, merged_lo if n == WOUT0 else None)
                if n > WOUT0:
                    sum_squares(n - 1 - WOUT0, DC)
            sum_squares(DC - 1, DC)

            h2_lo = merged_lo + DC

            def key_scores(c):
                pe.wait_ge(qf_ok, c + 1)
                if c >= 2:
                    pe.wait_ge(sc_ok, c - 1)
                for tt in range(TT):
                    last = nc.tensor.matmul(XB[c % 2][:, tt * P:(tt + 1) * P], qf[:, c % 2, tt * P:(tt + 1) * P],
                                            keys[:, c, :], start=True, stop=True)
                last.then_inc(ks_ok, 1)

            for c in range(2 * PH):
                n = WQ0 + c
                unit(n, act_hi, act_lo, h2_lo if c == 0 else None)
                if c == 0:
                    pe.wait_ge(keys_in, 16)
                if c >= 1:
                    key_scores(c - 1)
            key_scores(2 * PH - 1)
            pe.wait_ge(sc_ok, 2 * PH)

            def slab(t, per, b):
                q = t * per + b
                pe.wait_ge(w_split, q + (FRONT + 1))
                if isinstance(q, int) and q < 4:
                    pe.wait_ge(*sums_read(FRONT - 4 + q))
                else:
                    pe.wait_ge(ge_ok, q - 3)
                product(UB[b % 4][:, :], b % RING, range(DC), act_hi, act_lo).then_inc(w_used, 1)

            for q in range(4):
                slab(0, 4, q)
            with pe.Fori(1, (TOPK_UNITS + 4) // 4) as turn:
                for b in range(4):
                    slab(turn, 4, b)
            for q in range(TOPK_UNITS + 4, G_FIRST):
                slab(0, 4, q)
                tt, at_unit = divmod(q - TOPK_UNITS - 4, 4)
                if at_unit == 0 and tt < TT:
                    pe.wait_ge(ijw_ok, tt + 1)
                    if tt >= 2:
                        pe.wait_ge(ijt_cp, tt - 1)
                    for c in range(3):
                        last = nc.tensor.transpose(XB[tt % 2][:, c * P:(c + 1) * P], ijw[:, c, :], ident)
                    last.then_inc(ijt_ok, 1)
            pe.wait_ge(ijt_cp, TT)

            def g_turn(it, first):
                for b in range(G_UNITS):
                    slab(it, G_UNITS, G_FIRST + b)
                    for t in range(8 * b, 8 * b + 8):
                        j = t // 4
                        if t % 4 == 0 and not (first and j < 4):
                            pe.wait_ge(g_cp, it * (2 * TB // 4) + (j - 3))
                        pe.wait_ge(hot_ok, it * (4 * TB) + (2 * t + 2))
                        last = nc.tensor.matmul(bank[j % 4][:, (t % 4) * P:(t % 4 + 1) * P], hot[:, t % 8, 0, :],
                                                hot[:, t % 8, 1, :], start=True, stop=True)
                        if t % 4 == 3:
                            last.then_inc(g_ok, 1)

            g_turn(0, True)
            with pe.Fori(1, G_TURNS) as it:
                g_turn(it, False)
            with pe.Fori(G_LAST // 4, SLABS // 4) as turn:
                for b in range(4):
                    slab(turn, 4, b)

            pe.wait_ge(g_cp, T // 4)

            def v_slab(r, b, first=False, final=False):
                pe.wait_ge(w_split, r + (VBASE + 1))
                pe.wait_ge(c_lo, r + 1)
                for m in range(DC):
                    if first and m >= 4:
                        pe.wait_ge(ge_ok, SLABS - 7 + m)
                    w = slice(m * P, (m + 1) * P)
                    slot, c = b % RING, b % C_RING
                    nc.tensor.matmul(bank[m][:, :], w_hi[:, slot, w], mix_hi[:, c, :], start=first, stop=False)
                    nc.tensor.matmul(bank[m][:, :], w_hi[:, slot, w], mix_lo[:, c, :], start=False, stop=False)
                    last = nc.tensor.matmul(bank[m][:, :], w_lo[:, slot, w], mix_hi[:, c, :], start=False, stop=final)
                    if final and m < DC - 1:
                        last.then_inc(o_part, 1)
                last.then_inc(w_used, 1)

            for b in range(C_RING):
                v_slab(b, b, first=(b == 0))
            with pe.Fori(1, SLABS // C_RING - 1) as t:
                for b in range(C_RING):
                    v_slab(t * C_RING + b, b)
            for b in range(C_RING):
                v_slab(SLABS - C_RING + b, b, final=(b == C_RING - 1))


def layouts(i):
    f = lambda a: np.ascontiguousarray(np.asarray(a))

    def units(w):
        k, n = w.shape
        return w.reshape(k // P, P, n // P, P).transpose(2, 1, 0, 3).reshape(n // P, P, k)

    def cols(v):
        return np.asarray(v).reshape(-1, P).T

    w = {k: np.asarray(v) for k, v in i.items()}
    w_in = units(w["w_in"][0])
    w_mix = np.concatenate([units(w["w_conv_out"][0]), units(w["w_attn_out"][0])], axis=2)
    order = []
    for b in range(CC):
        order += [w_in[CC + b], w_in[b]]
    order += [w_in[8 + m] for m in range(12)]
    for kind in MIX:
        order.append(w_in[20 + DC * kind[2] + kind[1]] if kind[0] == "gate" else w_mix[kind[1]])
    order += list(units(w["w_out"][0])) + list(units(w["peer_wq"][0]))
    dw = w["conv_dw"][0].reshape(TAPS, CC, P).transpose(2, 1, 0).reshape(P, CC * TAPS)
    par = np.concatenate([cols(w["b_ada"][0]), cols(w["norm1_g"][0]), cols(w["norm2_g"][0]), dw,
                          cols(w["conv_b"][0]), cols(w["conv_ln_g"][0]), cols(w["conv_ln_b"][0]),
                          np.tile(w["q_norm_g"][0], 2)[:, None], np.tile(w["k_norm_g"][0], 2)[:, None]], axis=1)
    const = np.zeros((P, 5 * P), np.float32)
    const[:, 0:P] = np.eye(P)
    const[:, P:2 * P] = 1.0
    const[:, 2 * P:3 * P] = np.arange(P)
    for m in range(8):
        const[0:64, 3 * P + 16 * m + 2 * m] = 1.0
        const[64:128, 3 * P + 16 * m + 2 * m + 1] = 1.0
    const[:, 4 * P:4 * P + 16] = np.arange(16)
    selt = np.zeros((16, 8 * P), np.float32)
    for m in range(8):
        selt[2 * m, m * P:m * P + 64] = 1.0
        selt[2 * m + 1, m * P + 64:(m + 1) * P] = 1.0
    rel = np.clip(np.arange(P)[:, None] - np.arange(T)[None, :] + 384, -128, 128) + 128
    toep = w["rel_bias"][0][:, rel].transpose(1, 0, 2)
    keys = w["peer_keys"][0].reshape(2 * PH, NKEY, P).transpose(2, 0, 1)
    u = w["peer_u"][0].reshape(NKEY, NKEY, DC, P).transpose(1, 3, 2, 0).reshape(NKEY, P, D)
    v = w["peer_v"][0].reshape(NKEY, NKEY, D).transpose(1, 0, 2)
    return {
        "w_front": f(np.stack(order)), "w_ada": f(w["w_ada"][0].T.reshape(ADA, P, D)), "c": f(w["c"]), "par": f(par), "const": const,
        "selt": selt, "x": f(w["x"][0].T.reshape(DC, P, T)), "toep": f(toep), "keys": f(keys), "u": f(u), "v": f(v),
    }


def kernel(**inputs):
    import concourse.bacc as bacc
    from concourse.bass_utils import run_bass_kernel_spmd

    arrays = layouts(inputs)
    nc = bacc.Bacc("TRN2", target_bir_lowering=False, num_devices=1)
    aps = [nc.dram_tensor(f"{k}_dram", a.shape, F32, kind="ExternalInput").ap() for k, a in arrays.items()]
    g_d = nc.dram_tensor("g_scratch", (T // TB, P, NKEY * TB), F32, kind="Internal").ap()
    a_d = nc.dram_tensor("a_scratch", (SLABS, P, T), F32, kind="Internal").ap()
    out_d = nc.dram_tensor("out_dram", (DC, P, T), F32, kind="ExternalOutput").ap()
    block_program(nc, *aps, g_d, a_d, out_d)
    r = run_bass_kernel_spmd(nc, [{f"{k}_dram": a for k, a in arrays.items()}], core_ids=[0])
    return np.ascontiguousarray(r.results[0]["out_dram"].reshape(1, D, T).transpose(0, 2, 1))
```

```python
from contextlib import ExitStack

import numpy as np

import concourse.bass as bass
from concourse import mybir

ACT = mybir.ActivationFunctionType
ALU = mybir.AluOpType
AX = mybir.AxisListType
F32 = mybir.dt.float32
F32R = mybir.dt.float32r
U32 = mybir.dt.uint32

P = 128
T = 512
D = 1024
DC = D // P
TT = T // P
EPS = 1e-6
HEADS = 8
HD = 64
CHUNK = 64
TAPS = 31
CC = 4
PH = 8
TOPK = 16
NKEY = 128
LOWEST = -3.0e38
MASKED = -1e30
RING = 4

COL = {}
_at = 0
for _name, _n in (("b_ada", 6 * DC), ("g1", DC), ("g2", DC), ("dw", CC * TAPS), ("conv_b", CC),
                  ("ln_g", CC), ("ln_b", CC), ("qg", 1), ("kg", 1)):
    COL[_name] = (_at, _n)
    _at += _n
PAR_COLS = _at

GLU0, QK0, V0, MIX0 = 0, 8, 16, 20
MIX = []
for _m in range(DC):
    MIX += [("gate", _m, 0), ("gate", _m, 1)]
    if _m == 1:
        MIX += [("out", 0), ("out", 1)]
    if _m > 1:
        MIX += [("out", _m)]
WOUT0 = MIX0 + len(MIX)
WQ0 = WOUT0 + DC
FRONT = WQ0 + 2 * PH
SLABS = NKEY
VBASE = FRONT + SLABS
TB = 32
SC = 5
AHEAD = (7, 11, 15)
LAG = 3
ND = T - P
DT = ND // P
GT = DT
PICKS = PH * TOPK
EXP_SLAB = 19
LIST_SLABS = (26, 31, 37)
G_FIRST = 40
G_UNITS = 8
G_TURNS = ND // (2 * TB)
G_LAST = G_FIRST + G_TURNS * G_UNITS
POOL_FIRST, POOL_LAST = WQ0 + 2, FRONT + G_FIRST + 2
assert LIST_SLABS[-1] + 1 < G_FIRST and G_LAST < SLABS
EARLY_DOTS = 16
EARLY_SLAB = 24
EARLY_TURNS = 3
G_DOTS = 12
DOTS_A = EARLY_DOTS + G_TURNS * G_DOTS
LATE_TURNS = (SLABS - 4 - G_LAST) // 4
assert DOTS_A + 4 * (LATE_TURNS + 1) == PICKS
ACT_HOTS = (1, 3, 4, 6, 7)
C_RING = 8
C_LEAD = 3
ADA = 6 * DC
ADA_FIRST = 2 * DC


def block_program(nc, w_front, w_ada, c_d, par_d, const_d, selt_d, x_d, toep_d, keys_d, u_d, v_d, u_rows_d, g_d, a_d, x2_d, out_d):
    ctx = ExitStack()
    with ctx:
        def sb(name, shape, dt=F32):
            return ctx.enter_context(nc.sbuf_tensor("sb_" + name, shape, dt))

        def sem(name):
            return ctx.enter_context(nc.semaphore(name))

        w_hi = sb("w_hi", [P, RING, 1024], F32R)
        w_lo = sb("w_lo", [P, RING, 1024], F32R)
        act_hi = sb("act_hi", [P, DC, T], F32R)
        act_lo = sb("act_lo", [P, DC, T], F32R)
        mix_hi = sb("mix_hi", [P, DC, T], F32R)
        mix_lo = sb("mix_lo", [P, DC, T], F32R)
        stage = sb("stage", [P, RING, 1024])
        x = sb("x", [P, DC, T])
        wide = sb("wide", [P, DC, T])
        par = sb("par", [P, PAR_COLS])
        const = sb("const", [P, 5 * P])
        ones = sb("ones", [P, P])[:, :]
        htok = sb("htok", [P, D])
        selt = htok[0:16, :]
        mod = sb("mod", [P, ADA])
        small = sb("small", [P, 160])
        scr = sb("scr", [P, 13952])

        ident = const[:, 0:P]
        iota = const[:, P:2 * P]
        sel = const[:, 2 * P:3 * P].rearrange("p (m c) -> p m c", c=16)
        niota = const[:, 4 * P:5 * P]
        iota16 = const[:, 3 * P:3 * P + 16]

        def col(name, i=0, n=1):
            return par[:, COL[name][0] + i:COL[name][0] + i + n]

        def at(off, shape):
            n = int(np.prod(shape))
            v = scr[:, off:off + n]
            if len(shape) == 2:
                return v.rearrange("p (a b) -> p a b", b=shape[1])
            if len(shape) == 3:
                return v.rearrange("p (a b c) -> p a b c", b=shape[1], c=shape[2])
            return v

        vtok = at(0, [TT, 512])
        y = at(2048, [CC, T])
        U_W = TAPS - 1 + T
        u = at(4096, [CC, U_W])
        toep = at(6272, [2, T])
        r1 = 7296
        ada = at(r1, [4, 1024])
        ada2 = at(0, [2, 1024])
        cond2 = at(6272, [1024])
        pt = at(r1, [2, TT, T])
        gate = at(r1, [4, T])
        sq = at(11392, [2, T])
        rstd = at(12416, [T])
        cond = at(0, [1024])
        sqsum = (at(1024, [T]), at(10240, [T]))
        nrm, NS = at(11392, [5, T]), (0, 1, 3, 4)
        sc = at(11392, [SC, T])
        tmp = at(12928, [2, T])
        scores = at(0, [TT, 2 * PH, NKEY])
        keys = at(8192, [2 * PH, NKEY])
        qf = at(10240, [2, T])
        wf = wide[:, :, :].rearrange("p a b -> p (a b)")

        def wat(off, n):
            return wf[:, off:off + n]

        sv = wat(0, 1024).rearrange("p (t c k) -> p t c k", t=TT, c=16)
        si = wat(1024, 1024).bitcast(U32).rearrange("p (t c k) -> p t c k", t=TT, c=16)
        top = wat(2048, 512).rearrange("p (t h k) -> p t h k", t=TT, h=PH)
        pos = wat(2560, 512).bitcast(U32).rearrange("p (t h k) -> p t h k", t=TT, h=PH)
        ijw = wat(3072, 3 * P).rearrange("p (c k) -> p c k", c=3)
        rank = wat(3456, 2 * P).rearrange("p (c k) -> p c k", c=2)
        ranku = wat(3712, 2 * P).bitcast(U32).rearrange("p (c k) -> p c k", c=2)
        sif = at(12928, [256])
        hot16 = scr[:, 8192:8192 + 2048]
        mr = at(12928, [2, NKEY])
        cand = at(13184, [256])
        cand2 = at(13440, [256])
        gb = at(0, [2, NKEY, TB])
        hot = scr[:, 8192:8192 + 2048].rearrange("p (s a b) -> p s a b", s=8, a=2)
        ijt = at(10240, [3, ND])
        ga = at(11776, [2, ND])
        zsq = at(12544, [2, P])
        gtile = scr[:, 0:8 * ND].rearrange("p (s b j t) -> p s b j t", s=2, b=ND // TB, j=4)
        atile = at(8 * ND, [2, 4, ND])
        cf = at(8192, [2, ND])
        rows = x[:, :, :].rearrange("p (s a) t -> p s (a t)", s=4)
        acc = at(10240, [1024])
        idx3 = at(13184, [2, P]).bitcast(U32)
        w3 = at(13440, [P])
        dots = at(13568, [P])
        g3 = at(13696, [P])
        dot4 = at(13824, [4])
        idxc = at(13840, [4]).bitcast(U32)

        bank = [ctx.enter_context(nc.psum_tensor(f"bank{b}", [P, 512], F32)) for b in range(8)]
        SB = bank[0:4]
        STAT, XB = bank[1], (bank[2], bank[3])
        UB = bank[4:8]

        par_in = sem("par_in")
        ones_ok = sem("ones_ok")
        x_in = [sem(f"x_in{i}") for i in range(2)]
        selt_in = sem("selt_in")
        ada_in = [sem(f"ada_in{i}") for i in range(4)]
        ada2_in = [sem(f"ada2_in{i}") for i in range(2)]
        cond_in = sem("cond_in")
        w_in = [sem(f"w_in{i}") for i in range(RING)]
        toep_in = [sem(f"toep_in{i}") for i in range(2)]
        keys_in = sem("keys_in")
        gt_in = [sem(f"gt_in{i}") for i in range(2)]
        at_in = [sem(f"at_in{i}") for i in range(2)]
        a_out = [sem(f"a_out{i}") for i in range(2)]
        gw_out = [sem(f"gw_out{i}") for i in range(2)]
        out_in = [sem(f"out_in{i}") for i in range(2)]
        w_round = sem("w_round")
        w_split = sem("w_split")
        w_used = sem("w_used")
        cond_ok = sem("cond_ok")
        ada_used = sem("ada_used")
        mod_ok = sem("mod_ok")
        n_pre = sem("n_pre")
        sq_ok = sem("sq_ok")
        sa_ok = sem("sa_ok")
        sq_used = sem("sq_used")
        ms_ok = sem("ms_ok")
        rt_early = sem("rt_early")
        rt_ok = sem("rt_ok")
        a_pre = sem("a_pre")
        a_hi = sem("a_hi")
        a_lo = sem("a_lo")
        step = sem("step")
        tap_ok = sem("tap_ok")
        sig_ok = sem("sig_ok")
        u_ok = sem("u_ok")
        qk_ok = sem("qk_ok")
        rb_ok = sem("rb_ok")
        qkn_ok = sem("qkn_ok")
        v_sum = sem("v_sum")
        v_ok = sem("v_ok")
        msk_ok = sem("msk_ok")
        s_ok = sem("s_ok")
        sb_ok = sem("sb_ok")
        e_ok = sem("e_ok")
        ri_ok = sem("ri_ok")
        p_ok = sem("p_ok")
        t_ok = sem("t_ok")
        pt_ok = sem("pt_ok")
        o_ok = sem("o_ok")
        conv_ok = sem("conv_ok")
        y_sum = sem("y_sum")
        y_ok = sem("y_ok")
        y_act = sem("y_act")
        y_nrm = sem("y_nrm")
        m_ok = sem("m_ok")
        x2_ok = sem("x2_ok")
        qf_ok = sem("qf_ok")
        ks_ok = sem("ks_ok")
        sc_ok = sem("sc_ok")
        tk_ok = sem("tk_ok")
        te_ok = sem("te_ok")
        ijw_ok = sem("ijw_ok")
        ijt_ok = sem("ijt_ok")
        ijt_cp = sem("ijt_cp")
        hot_ok = sem("hot_ok")
        g_ok = sem("g_ok")
        g_cp = sem("g_cp")
        ge_ok = sem("ge_ok")
        c_mul = sem("c_mul")
        c_hi = sem("c_hi")
        c_lo = sem("c_lo")
        ht_ok = sem("ht_ok")
        ht_cp = sem("ht_cp")
        x2_out = sem("x2_out")
        x2_in = sem("x2_in")
        idx_ok = sem("idx_ok")
        col_ok = sem("col_ok")
        row_in = [sem(f"row_in{i}") for i in range(4)]
        dot_ok = sem("dot_ok")
        d4_ok = sem("d4_ok")
        g3_ok = sem("g3_ok")
        acc_ok = sem("acc_ok")
        z_ok = sem("z_ok")
        hotw_ok = sem("hotw_ok")
        t3_ok = sem("t3_ok")
        fin_ok = sem("fin_ok")

        def sums_read(n):
            if n < QK0:
                return (sig_ok if n % 2 == 0 else u_ok), n // 2 + 1
            if n < V0:
                return sq_ok, DC + n - QK0 + 1
            if n < MIX0:
                return v_ok, n - V0 + 1
            if n < WOUT0:
                kind = MIX[n - MIX0]
                return (m_ok, kind[1] + 1) if kind[0] == "out" else (sig_ok, CC + 2 * kind[1] + kind[2] + 1)
            return (x2_ok, n - WOUT0 + 1) if n < WQ0 else (qf_ok, n - WQ0 + 1)

        block = ctx.enter_context(nc.Block())

        @block.sync
        def _(sp):
            for i in range(2):
                half = slice(i * DC // 2, (i + 1) * DC // 2)
                sp.dma_start(x[:, half, :], x_d[half].rearrange("c p t -> p c t")).then_inc(x_in[i], 16)

            def load(n, slot, src):
                if not isinstance(n, int) or n >= RING:
                    sp.wait_ge(w_split, n - RING + 1)
                return sp.dma_start(stage[:, slot, :], src.rearrange("a p n -> p (a n)"))

            for n in range(ADA_FIRST):
                if n >= 4:
                    sp.wait_ge(ada_used, n - 3)
                sp.dma_start(ada[:, n % 4, :], w_ada[n]).then_inc(ada_in[n % 4], 16)
                if n in (3, 5):
                    slot = (n - 3) // 2
                    load(slot, slot, w_front[slot:slot + 1]).then_inc(w_in[slot], 16)
            for n in range(2, RING):
                load(n, n, w_front[n:n + 1]).then_inc(w_in[n], 16)
            with sp.Fori(1, FRONT // RING) as turn:
                for slot in range(RING):
                    load(turn * RING + slot, slot, w_front[bass.ds(turn * RING + slot, 1)]).then_inc(w_in[slot], 16)
            with sp.Fori(0, SLABS // RING) as turn:
                for slot in range(RING):
                    load(turn * RING + (FRONT + slot), slot, u_d[bass.ds(turn * RING + slot, 1)]).then_inc(w_in[slot], 16)

            def slab_load(k, s, first=False):
                if not first:
                    sp.wait_ge(c_mul, k * 4 - 4)
                for i in range(2):
                    sp.wait_ge(a_out[i], k * 32 + 32)
                sp.dma_start(gtile[:, s, :, :, :].rearrange("p b j t -> p b (j t)"),
                             g_d[:, :, bass.ds(k * 4 * TB, 4 * TB)].rearrange("b p n -> p b n")
                             ).then_inc(gt_in[s], 16)
                sp.dma_start(atile[:, s, :, :], a_d[bass.ds(k * 4, 4)].rearrange("a p t -> p a t")
                             ).then_inc(at_in[s], 16)

            for s in range(2):
                sp.wait_ge(gw_out[s], 16 * G_TURNS)
            slab_load(0, 0, True)

            def v_loads(half, s):
                for slot in range(RING):
                    load(half * RING + (VBASE + slot), slot, v_d[bass.ds(half * RING + slot, 1)]).then_inc(w_in[slot], 16)
                if s is not None:
                    slab_load(half + 1, s)

            v_loads(0, None)
            slab_load(1, 1, True)
            with sp.Fori(0, SLABS // RING // 2 - 1) as tt2:
                v_loads(tt2 * 2 + 1, 0)
                v_loads(tt2 * 2 + 2, 1)
            v_loads(SLABS // RING - 1, None)
            sp.dma_start(wide[:, :, :], x2_d.rearrange("c p t -> p c t")).then_inc(x2_in, 16)
            for m in range(DC):
                sp.wait_ge(fin_ok, m + 1)
                sp.dma_start(out_d[m], wide[:, m, :]).then_inc(out_in[m % 2], 16)
            for i in range(2):
                sp.wait_ge(out_in[i], 16 * DC // 2)

        @block.gpsimd
        def _(pool):
            nc.gpsimd.memset(u[:, :, 0:TAPS - 1], 0.0).then_inc(msk_ok, 1)
            for n in range(2):
                pool.wait_ge(w_round, n + 1)
                nc.gpsimd.tensor_tensor(w_lo[:, n, :], stage[:, n, :], w_hi[:, n, :].bitcast(F32),
                                        ALU.subtract).then_inc(w_split, 1)
            for m in range(DC):
                pool.wait_ge(a_hi, m + 1)
                nc.gpsimd.tensor_tensor(act_lo[:, m, :], nrm[:, NS[m % 4], :], act_hi[:, m, :].bitcast(F32),
                                        ALU.subtract).then_inc(a_lo, 1)
            for h in range(HEADS):
                if h >= 2:
                    pool.wait_ge(sb_ok, TT * (h - 1))
                pool.dma_start(toep[:, h % 2, :], toep_d[:, h, :]).then_inc(toep_in[h % 2], 16)
                pool.wait_ge(toep_in[h % 2], 16 * (h // 2 + 1))
                nc.gpsimd.memset(toep[0:CHUNK, h % 2, T - CHUNK:T], MASKED).then_inc(msk_ok, 1)
            pool.wait_ge(o_ok, HEADS)
            for n in range(ADA_FIRST, ADA):
                if n >= ADA_FIRST + 2:
                    pool.wait_ge(ada_used, n - 1)
                pool.dma_start(ada2[:, n % 2, :], w_ada[n]).then_inc(ada2_in[n % 2], 16)
            pool.wait_ge(m_ok, DC)
            pool.dma_start(keys[:, :, :], keys_d).then_inc(keys_in, 16)

            def split_unit(n, slot):
                pool.wait_ge(w_round, n + 1)
                if isinstance(n, int):
                    pool.wait_ge(w_split, n)
                else:
                    pool.nop(nofuse=True)
                nc.gpsimd.tensor_tensor(w_lo[:, slot, :], stage[:, slot, :], w_hi[:, slot, :].bitcast(F32),
                                        ALU.subtract).then_inc(w_split, 1)

            for n in range(POOL_FIRST, WQ0 + 4):
                split_unit(n, n % RING)
            pool.wait_ge(a_pre, 2 * DC)
            pool.dma_start(x2_d.rearrange("c p t -> p c t"), x[:, :, :]).then_inc(x2_out, 16)
            with pool.Fori(WQ0 // RING + 1, (FRONT + EARLY_SLAB) // RING) as turn:
                for slot in range(RING):
                    split_unit(turn * RING + slot, slot)
            pool.wait_ge(x2_out, 16)
            pool.wait_ge(idx_ok, 1)

            def gather(which, k, b, table):
                nc.gpsimd.tensor_copy(idxc[:, b:b + 1], idx3[:, which, bass.ds(k, 1)]).then_inc(col_ok, 1)
                pool.wait_ge(col_ok, k + (which * PICKS + 1))
                pool.nop(nofuse=True)
                pool.indirect_dma_start(rows[:, b, :], None, table,
                                        bass.IndirectOffsetOnAxis(ap=idxc[:, b:b + 1], axis=0)
                                        ).then_inc(row_in[b], 16)

            for b in range(4):
                split_unit(FRONT + EARLY_SLAB + b, b)
                gather(0, b, b, u_rows_d)

            def u_gather(t, b):
                pool.wait_ge(dot_ok, t * 4 + (b - 3))
                gather(0, t * 4 + b, b, u_rows_d)

            with pool.Fori(1, EARLY_TURNS) as t:
                for b in range(4):
                    split_unit(t * 4 + (FRONT + EARLY_SLAB + b), b)
                    u_gather(t, b)
            for n in range(FRONT + EARLY_SLAB + 4 * EARLY_TURNS, POOL_LAST - 2):
                split_unit(n, n % RING)
            for b in range(4):
                u_gather(EARLY_TURNS, b)
                if b % 2:
                    split_unit(POOL_LAST - 2 + b // 2, (POOL_LAST - 2 + b // 2) % RING)
            with pool.Fori(EARLY_TURNS + 1, PICKS // 4) as t:
                for b in range(4):
                    u_gather(t, b)
            v_rows_d = v_d.rearrange("j i d -> (j i) d")
            for b in range(4):
                pool.wait_ge(dot_ok, PICKS - 3 + b)
                gather(1, b, b, v_rows_d)

            def late_gathers(t):
                for b in range(4):
                    pool.wait_ge(acc_ok, t * 4 + (b - 2))
                    gather(1, t * 4 + b, b, v_rows_d)

            with pool.Fori(1, PICKS // 4) as t:
                late_gathers(t)

        def round_unit(act, n, slot):
            act.wait_ge(w_in[slot], 16 * (n // RING + 1) if isinstance(n, int) else n[1])
            nn = n if isinstance(n, int) else n[0]
            if not isinstance(n, int) or n >= RING:
                act.wait_ge(w_used, nn - RING + 1)
            nc.scalar.activation(w_hi[:, slot, :], stage[:, slot, :], ACT.Copy).then_inc(w_round, 1)

        @block.scalar
        def _(act):
            act.dma_start(cond, c_d.to_broadcast([P, D])).then_inc(cond_in, 16)
            act.dma_start(par[:, :], par_d).then_inc(par_in, 16)
            act.dma_start(const[:, :], const_d).then_inc(par_in, 16)
            act.dma_start(selt, selt_d).then_inc(selt_in, 16)
            act.wait_ge(cond_in, 16)
            nc.scalar.activation(cond, cond, ACT.Silu).then_inc(cond_ok, 1)
            squares = 0

            def square(src, used):
                nonlocal squares
                if used > 0:
                    act.wait_ge(sq_used, used)
                nc.scalar.activation(sq[:, squares % 2, :], src, ACT.Square).then_inc(sq_ok, 1)
                squares += 1

            def norm_square(m, k):
                if m >= 2:
                    act.wait_ge(sa_ok, k * (DC - 2) + max(m - 2, 1))
                square(x[:, m, :], squares - 1 if m < 2 else 0)

            for m in range(DC):
                if m % (DC // 2) == 0:
                    act.wait_ge(x_in[m // (DC // 2)], 16)
                norm_square(m, 0)
            act.wait_ge(ones_ok, 1)
            nc.scalar.activation(small[:, 42:43], ones[:, 0:1], ACT.Sqrt).then_inc(rt_early, 1)
            act.wait_ge(ms_ok, 1)
            nc.scalar.activation(rstd, rstd, ACT.Sqrt).then_inc(rt_ok, 1)
            for n in range(2):
                round_unit(act, n, n % RING)
            hi = 0

            def norm_chunk(m, done, scale, shift):
                nonlocal hi
                act.wait_ge(n_pre, done + m + 1)
                nc.scalar.activation(nrm[:, NS[m % 4], :], nrm[:, NS[m % 4], :], ACT.Identity, scale=scale, bias=shift
                                     ).then_inc(a_pre, 1)
                act.wait_ge(a_pre, done + m + 1)
                nc.scalar.activation(act_hi[:, m, :], nrm[:, NS[m % 4], :], ACT.Copy).then_inc(a_hi, 1)
                hi += 1

            for m in range(DC):
                act.wait_ge(mod_ok, m + 1)
                norm_chunk(m, 0, small[:, 8 + m:9 + m], mod[:, m:m + 1])
            round_unit(act, 2, 2)

            def evac(n):
                pb = UB[n % 4][:, :]
                act.wait_ge(w_used, n + 1)
                if n < QK0:
                    if n % 2 == 0:
                        i = n // 2
                        if i >= 2:
                            act.wait_ge(u_ok, i - 1)
                        nc.scalar.activation(tmp[:, i % 2, :], pb, ACT.Sigmoid).then_inc(sig_ok, 1)
                elif n < V0:
                    nc.scalar.activation(wide[:, n - QK0, :], pb, ACT.Copy).then_inc(qk_ok, 1)
                    square(pb, squares - 1)
            for n in range(V0 + 1):
                if n >= 1:
                    evac(n - 1)
                round_unit(act, n + 3, (n + 3) % RING)
            act.wait_ge(ms_ok, 2)
            nc.scalar.activation(rstd[0:16, :], rstd[0:16, :], ACT.Sqrt).then_inc(rt_ok, 1)
            for tt in range(TT):
                if tt < TT - 1:
                    act.wait_ge(v_sum, tt + 1)
                else:
                    act.wait_ge(w_used, MIX0)
                nc.scalar.activation(vtok[:, tt, :], UB[tt][:, :], ACT.Copy).then_inc(v_ok, 1)

            for s in range(HEADS * TT + LAG + 1):
                if s < HEADS * TT:
                    n = (s % TT + 1) * P
                    act.wait_ge(sb_ok, s + 1)
                    nc.scalar.activation(sc[:, s % SC, 0:n], sc[:, s % SC, 0:n], ACT.Exp,
                                         bias=small[:, 120 + s % 8:121 + s % 8],
                                         accum_out=small[:, 128 + s % 8:129 + s % 8]).then_inc(e_ok, 1)
                r = s - 1
                if 0 <= r < HEADS * TT:
                    n = (r % TT + 1) * P
                    act.wait_ge(ri_ok, r + 1)
                    nc.scalar.activation(sc[:, r % SC, 0:n], sc[:, r % SC, 0:n], ACT.Copy,
                                         scale=small[:, 136 + r % 8:137 + r % 8]).then_inc(p_ok, 1)
                if s in AHEAD:
                    round_unit(act, MIX0 + AHEAD.index(s), (MIX0 + AHEAD.index(s)) % RING)
                r = s - LAG
                if 0 <= r < HEADS * TT:
                    h, q = divmod(r, TT)
                    if h >= 2:
                        act.wait_ge(o_ok, h - 1)
                    act.wait_ge(t_ok, r + 1)
                    n = (q + 1) * P
                    nc.scalar.activation(pt[:, h % 2, 0:q + 1, q * P:(q + 1) * P],
                                         UB[r % 2][:, 0:n].rearrange("p (b q) -> p b q", q=P),
                                         ACT.Copy).then_inc(pt_ok, 1)
                if r in (2 * TT, 4 * TT, 6 * TT):
                    pair = r // (2 * TT) - 1
                    act.wait_ge(o_ok, 2 * pair + 2)
                    nc.scalar.activation(mix_hi[:, CC + pair, :], UB[2 + pair % 2][:, :], ACT.Copy).then_inc(a_hi, 1)
                    hi += 1
            act.wait_ge(o_ok, HEADS)
            nc.scalar.activation(mix_hi[:, CC + 3, :], UB[3][:, :], ACT.Copy).then_inc(a_hi, 1)
            hi += 1

            act.dma_start(cond2, c_d.to_broadcast([P, D])).then_inc(cond_in, 16)
            act.wait_ge(cond_in, 32)
            nc.scalar.activation(cond2, cond2, ACT.Silu).then_inc(cond_ok, 1)

            def mix_evac(n):
                kind = MIX[n - MIX0]
                if kind[0] == "gate":
                    _, m, br = kind
                    act.wait_ge(w_used, n + 1)
                    if m >= 2:
                        act.wait_ge(m_ok, m - 1)
                    nc.scalar.activation(gate[:, 2 * (m % 2) + br, :], UB[n % 4][:, :], ACT.Sigmoid).then_inc(sig_ok, 1)

            for n in range(MIX0, WOUT0):
                if n > MIX0:
                    mix_evac(n - 1)
                round_unit(act, n + 3, (n + 3) % RING)
                if n == MIX0:
                    for i in range(CC):
                        act.wait_ge(y_ok, i + 1)
                        square(y[:, i, :], squares - 1)
                    act.wait_ge(ms_ok, 4)
                    nc.scalar.activation(rstd, rstd, ACT.Sqrt).then_inc(rt_ok, 1)
                if n == MIX0 + 2:
                    for i in range(CC):
                        act.wait_ge(y_nrm, i + 1)
                        nc.scalar.activation(y[:, i, :], y[:, i, :], ACT.Silu, scale=col("ln_g", i),
                                             bias=col("ln_b", i)).then_inc(y_act, 1)
                        act.wait_ge(y_act, i + 1)
                        nc.scalar.activation(mix_hi[:, i, :], y[:, i, :], ACT.Copy).then_inc(a_hi, 1)
                        hi += 1

            def merged_round(m):
                nonlocal hi
                if m == 0:
                    act.wait_ge(w_used, WOUT0 - 1)
                act.wait_ge(m_ok, m + 1)
                nc.scalar.activation(act_hi[:, m, :], wide[:, m, :], ACT.Copy).then_inc(a_hi, 1)
                hi += 1

            for m in range(DC):
                merged_round(m)
            for n in range(WOUT0, WQ0):
                m = n - WOUT0 - 1
                if m >= 0:
                    act.wait_ge(x2_ok, m + 1)
                    norm_square(m, 1)
                round_unit(act, n + 3, (n + 3) % RING)
            nc.scalar.activation(small[:, 43:44], ones[:, 0:1], ACT.Sqrt).then_inc(rt_early, 1)
            act.wait_ge(x2_ok, DC)
            norm_square(DC - 1, 1)
            act.wait_ge(ms_ok, 5)
            nc.scalar.activation(rstd, rstd, ACT.Sqrt).then_inc(rt_ok, 1)
            for m in range(DC):
                norm_chunk(m, DC, small[:, 16 + m:17 + m], mod[:, 3 * DC + m:3 * DC + m + 1])
                if m in (5, DC - 1):
                    half = int(m == DC - 1)
                    act.wait_ge(ht_ok, 4 * half + 4)
                    nc.scalar.activation(htok[:, half * 512:half * 512 + 512], XB[half][:, :], ACT.Copy).then_inc(ht_cp, 1)

            def wq_evac(c):
                n = WQ0 + c
                act.wait_ge(w_used, n + 1)
                if c >= 2:
                    act.wait_ge(ks_ok, c - 1)
                nc.scalar.activation(qf[:, c % 2, :], UB[n % 4][:, :], ACT.Copy).then_inc(qf_ok, 1)

            def ks_evac(c):
                act.wait_ge(ks_ok, c + 1)
                nc.scalar.activation(scores[:, :, c, :], XB[c % 2][:, :].rearrange("p (t k) -> p t k", t=TT),
                                     ACT.Copy).then_inc(sc_ok, 1)

            for c in range(2 * PH):
                if c >= 1:
                    wq_evac(c - 1)
                round_unit(act, WQ0 + c + 3, (WQ0 + c + 3) % RING)
                if c >= 2:
                    ks_evac(c - 2)
            wq_evac(2 * PH - 1)
            ks_evac(2 * PH - 2)
            ks_evac(2 * PH - 1)
            def slab(t, per, b, first=False):
                q = t * per + b
                if not first:
                    k = (b - 1) % 4
                    act.wait_ge(w_used, q + FRONT)
                    if not isinstance(q, int) or q >= 3:
                        act.wait_ge(a_out[k % 2], (t * (per // 2) + (b - 1) // 2) * 16)
                    nc.scalar.activation(ga[:, k % 2, :], UB[k][:, 0:ND], ACT.Gelu).then_inc(ge_ok, 1)
                turns = t * (per // 4) + (FRONT // RING + 1 + (b + 3) // 4)
                round_unit(act, (q + (FRONT + 3), turns * 16), (b + 3) % RING)
                if not first:
                    act.wait_ge(ge_ok, q)
                    src, dst = ga[:, k % 2, :], a_d[bass.ds(q - 1, 1)].rearrange("a p t -> p (a t)")
                    act.dma_start(dst, src).then_inc(a_out[k % 2], 16)

            for q in range(G_FIRST):
                slab(0, 4, q, q == 0)
                if q == EXP_SLAB:
                    for tt in range(TT):
                        act.wait_ge(tk_ok, tt + 1)
                        v = top[:, tt, :, :].rearrange("p h k -> p (h k)")
                        nc.scalar.activation(v, v, ACT.Exp).then_inc(te_ok, 1)
                if q - 1 in LIST_SLABS:
                    tt = LIST_SLABS.index(q - 1)
                    act.wait_ge(ijt_ok, tt + 1)
                    for c in range(3):
                        nc.scalar.activation(ijt[:, c, tt * P:(tt + 1) * P], XB[tt % 2][:, c * P:(c + 1) * P],
                                             ACT.Copy, scale=-1.0 if c == 1 else 1.0).then_inc(ijt_cp, 1)

            def g_turn(it, first):
                n_hot = len(ACT_HOTS)
                for b in range(G_UNITS):
                    for c0 in range(0, n_hot, 2):
                        some = range(c0, min(c0 + 2, n_hot))
                        for c in some:
                            if not (first and b == 0):
                                act.wait_ge(g_ok, it * (2 * TB // 4) + (2 * b + ACT_HOTS[c] // 4 - 1))
                            jcol = ijt[:, 1, bass.ds(it * (2 * TB) + (8 * b + ACT_HOTS[c]), 1)]
                            if not (first and b == 0 and c < 2):
                                act.wait_ge(hotw_ok, it * (n_hot * G_UNITS) + (b * n_hot + c - 1))
                            nc.scalar.activation(zsq[:, (b * n_hot + c) % 2, :], iota, ACT.Square, bias=jcol
                                                 ).then_inc(z_ok, 1)
                        for c in some:
                            wcol = ijt[:, 2, bass.ds(it * (2 * TB) + (8 * b + ACT_HOTS[c]), 1)]
                            act.wait_ge(z_ok, it * (n_hot * G_UNITS) + (b * n_hot + c + 1))
                            nc.scalar.activation(hot[:, ACT_HOTS[c], 1, :], zsq[:, (b * n_hot + c) % 2, :], ACT.Relu,
                                                 scale=-4.0, bias=wcol).then_inc(hotw_ok, 1)
                    slab(it, G_UNITS, G_FIRST + b)
                    for j in (2 * b, 2 * b + 1):
                        s, o = divmod(4 * j, TB)
                        if o == 0 and not first:
                            act.wait_ge(gw_out[s], it * 16)
                        act.wait_ge(g_ok, it * (2 * TB // 4) + (j + 1))
                        nc.scalar.activation(gb[:, s, :, o:o + 4].rearrange("p j t -> p t j"),
                                             bank[j % 4][:, :].rearrange("p (t j) -> p t j", t=4),
                                             ACT.Copy).then_inc(g_cp, 1)
                        if o == TB - 4:
                            act.wait_ge(g_cp, it * (2 * TB // 4) + (j + 1))
                            act.dma_start(g_d[bass.ds(it * 2 + s, 1)].rearrange("a p n -> p (a n)"),
                                          gb[:, s, :, :].rearrange("p j t -> p (j t)")).then_inc(gw_out[s], 16)

            g_turn(0, True)
            with act.Fori(1, G_TURNS) as it:
                g_turn(it, False)
            with act.Fori(G_LAST // 4, SLABS // 4 - 1) as turn:
                for b in range(4):
                    slab(turn, 4, b)

            def coefficients(r, b):
                act.wait_ge(c_mul, r + 1)
                act.wait_ge(w_used, r + (VBASE - C_RING + 1))
                nc.scalar.activation(mix_hi[:, b % C_RING, 0:ND], cf[:, b % 2, :], ACT.Copy).then_inc(c_hi, 1)

            for b in range(4):
                slab(SLABS // 4 - 1, 4, b)
                if b:
                    coefficients(b - 1, b - 1)
                if b == 2:
                    act.wait_ge(d4_ok, PICKS // 4)
                    nc.scalar.activation(g3, dots, ACT.Gelu).then_inc(g3_ok, 1)

            def v_turn(t, last):
                for b in range(C_RING):
                    r = t * C_RING + b
                    if isinstance(t, int) and r == 0:
                        slab_end()
                    if not (last and b + 3 >= C_RING):
                        turns = t * 2 + (VBASE // RING + 1 + (b + 3) // 4)
                        round_unit(act, (r + (VBASE + 3), turns * 16), (b + 3) % RING)
                    if not (last and b + C_LEAD >= C_RING):
                        coefficients(r + C_LEAD, b + C_LEAD)

            def slab_end():
                act.wait_ge(w_used, VBASE)
                act.wait_ge(a_out[1], 16 * (SLABS // 2 - 1))
                nc.scalar.activation(ga[:, 1, :], UB[3][:, 0:ND], ACT.Gelu).then_inc(ge_ok, 1)
                act.wait_ge(ge_ok, SLABS)
                act.dma_start(a_d[SLABS - 1], ga[:, 1, :]).then_inc(a_out[1], 16)

            v_turn(0, False)
            with act.Fori(1, SLABS // C_RING - 1) as t:
                v_turn(t, False)
            v_turn(SLABS // C_RING - 1, True)

        @block.vector
        def _(dve):
            count = {"step": 0}

            def link(ins):
                count["step"] += 1
                ins.then_inc(step, 1)
                dve.wait_ge(step, count["step"])

            def mark(ins):
                count["step"] += 1
                ins.then_inc(step, 1)
                return count["step"]

            def split_unit(n, slot):
                dve.wait_ge(w_round, n + 1)
                nc.vector.tensor_tensor(w_lo[:, slot, :], stage[:, slot, :], w_hi[:, slot, :].bitcast(F32),
                                        ALU.subtract).then_inc(w_split, 1)

            lo = 0

            def lo_part(dst, src, hi_ap):
                nonlocal lo
                dve.wait_ge(a_hi, lo + 1)
                nc.vector.tensor_tensor(dst, src, hi_ap.bitcast(F32), ALU.subtract).then_inc(a_lo, 1)
                lo += 1

            def ada_unit(n, src, by, arrived, value):
                dve.wait_ge(arrived, value)
                nc.vector.tensor_tensor_reduce(src, src, by, 1.0, 0.0, ALU.mult, ALU.add,
                                               mod[:, n:n + 1]).then_inc(ada_used, 1)

            def ada_rest(n):
                if n == ADA_FIRST:
                    dve.wait_ge(cond_ok, 2)
                ada_unit(n, ada2[:, n % 2, :], cond2, ada2_in[n % 2], 16 * ((n - ADA_FIRST) // 2 + 1))

            nc.vector.memset(ones, 1.0).then_inc(ones_ok, 1)

            def ada_first(n):
                c = n // 2 if n % 2 else DC + n // 2
                ada_unit(c, ada[:, n % 4, :], cond, ada_in[n % 4], 16 * (n // 4 + 1))

            def add_squares(m, k):
                seen = k * (DC - 2) + m - 1
                dve.wait_ge(sq_ok, k * (2 * DC + CC) + m + 1)
                if m >= 2:
                    dve.wait_ge(sa_ok, seen)
                nc.vector.tensor_tensor(sqsum[k], sq[:, 0, :] if m == 1 else sqsum[k], sq[:, m % 2, :], ALU.add
                                        ).then_inc(sa_ok, 1)

            for m in range(1, DC - 1):
                add_squares(m, 0)
            dve.wait_ge(cond_ok, 1)
            for n in range(3):
                ada_first(n)
            dve.wait_ge(par_in, 32)
            link(nc.vector.tensor_scalar(small[:, 40:41], col("qg"), HD ** -0.5, None, ALU.mult))

            def norm_scale(width):
                count["ms"] = count.get("ms", 0) + 1
                nc.vector.tensor_scalar(rstd, STAT[:, :], 1.0 / width, EPS, ALU.mult, ALU.add).then_inc(ms_ok, 1)
                dve.wait_ge(rt_ok, count["ms"])
                link(nc.vector.reciprocal(rstd, rstd))

            def normalised(first, beside):
                norm_scale(D)
                base = lo
                for m in range(DC + 2):
                    if m < DC:
                        if m >= 4:
                            dve.wait_ge(a_lo, base + m - 3)
                            if not first:
                                dve.wait_ge(ht_ok, m - 3)
                        nc.vector.tensor_tensor(nrm[:, NS[m % 4], :], x[:, m, :], rstd, ALU.mult).then_inc(n_pre, 1)
                    if m >= 2 and not first:
                        lo_part(act_lo[:, m - 2, :], nrm[:, NS[(m - 2) % 4], :], act_hi[:, m - 2, :])
                    beside(m)

            link(nc.vector.tensor_scalar(small[:, 48:48 + DC], col("b_ada", DC, DC), 1.0, None, ALU.add))

            def first_norm(m):
                if m < DC:
                    for n in (2 * m, 2 * m + 1):
                        if n >= 3:
                            ada_first(n)
                    dve.wait_ge(ada_used, 2 * m + 2)
                    mark(nc.vector.scalar_tensor_tensor(out=small[:, 8 + m:9 + m], in0=mod[:, DC + m:DC + m + 1],
                                                        scalar=small[:, 48 + m:49 + m], in1=col("g1", m),
                                                        op0=ALU.add, op1=ALU.mult))
                    nc.vector.tensor_tensor(mod[:, m:m + 1], mod[:, m:m + 1], col("b_ada", m), ALU.add
                                            ).then_inc(mod_ok, 1)

            dve.wait_ge(sq_used, DC)
            normalised(True, first_norm)
            lo += DC
            dve.wait_ge(a_lo, lo)

            def conv(first, n):
                for k in range(first, min(first + n, CC * TAPS)):
                    pair, k2 = divmod(k, 2 * TAPS)
                    w, i = k2 // 2, 2 * pair + k2 % 2
                    src, wt = u[:, i, w:w + T], col("dw", i * TAPS + w)
                    if w == 0:
                        dve.wait_ge(u_ok, i + 1)
                        dve.wait_ge(msk_ok, 1)
                        ins = nc.vector.tensor_scalar(y[:, i, :], src, wt, col("conv_b", i), ALU.mult, ALU.add)
                    else:
                        dve.wait_ge(tap_ok, k - 1)
                        ins = nc.vector.scalar_tensor_tensor(out=y[:, i, :], in0=src, scalar=wt, in1=y[:, i, :],
                                                             op0=ALU.mult, op1=ALU.add)
                    ins.then_inc(tap_ok, 1)
                return first + n

            done = 0

            dve.wait_ge(w_split, 2)
            for n in range(MIX0):
                if n <= V0:
                    split_unit(n + 2, (n + 2) % RING)
                if n == V0:
                    split_unit(n + 3, (n + 3) % RING)
                j = n - 1
                if 0 <= j < QK0 and j % 2 == 1:
                    i = j // 2
                    dve.wait_ge(w_used, j + 1)
                    dve.wait_ge(sig_ok, i + 1)
                    nc.vector.tensor_tensor(u[:, i, TAPS - 1:], tmp[:, i % 2, :], UB[j % 4][:, :],
                                            ALU.mult).then_inc(u_ok, 1)
                if n == V0:
                    dve.wait_ge(sq_used, 2 * DC)
                    count["ms"] += 1
                    nc.vector.tensor_scalar(rstd[0:16, :], STAT[0:16, :], 1.0 / HD, EPS, ALU.mult, ALU.add
                                            ).then_inc(ms_ok, 1)
                    dve.wait_ge(rt_ok, 2)
                    nc.vector.reciprocal(rstd[0:16, :], rstd[0:16, :]).then_inc(ms_ok, 1)
                if n > V0:
                    for m in range((n - V0 - 1) * 3, min((n - V0) * 3, 8)):
                        dve.wait_ge(rb_ok, m + 1)
                        dve.wait_ge(qk_ok, m + 1)
                        nc.vector.scalar_tensor_tensor(out=wide[:, m, :], in0=wide[:, m, :],
                                                       scalar=small[:, 40:41] if m < 4 else col("kg"),
                                                       in1=XB[m % 2][:, :], op0=ALU.mult, op1=ALU.mult
                                                       ).then_inc(qkn_ok, 1)
                if 4 <= n < MIX0 - 1:
                    done = conv(done, 6 if n < V0 else 5)

            def o_lo(pair):
                nonlocal lo
                dve.wait_ge(a_hi, lo + 1)
                nc.vector.tensor_tensor(mix_lo[:, CC + pair, :], UB[2 + pair % 2][:, :],
                                        mix_hi[:, CC + pair, :].bitcast(F32), ALU.subtract).then_inc(a_lo, 1)
                lo += 1

            for s in range(HEADS * TT + 1):
                if s < HEADS * TT:
                    h, q = divmod(s, TT)
                    n = (q + 1) * P
                    if s >= SC:
                        dve.wait_ge(t_ok, s - SC + 1)
                    dve.wait_ge(s_ok, s + 1)
                    dve.wait_ge(msk_ok, h + 2)
                    link(nc.vector.tensor_tensor_reduce(sc[:, s % SC, 0:n], SB[s % 4][:, 0:n],
                                                        toep[:, h % 2, T - n:T], 1.0, LOWEST, ALU.add, ALU.max,
                                                        small[:, 112 + s % 8:113 + s % 8]))
                    nc.vector.tensor_scalar(small[:, 120 + s % 8:121 + s % 8], small[:, 112 + s % 8:113 + s % 8], -1.0,
                                            None, ALU.mult).then_inc(sb_ok, 1)
                r = s - 1
                if r >= 0:
                    n = (r % TT + 1) * P
                    dve.wait_ge(e_ok, r + 1)
                    nc.vector.reciprocal(small[:, 136 + r % 8:137 + r % 8], small[:, 128 + r % 8:129 + r % 8]
                                         ).then_inc(ri_ok, 1)
                done = conv(done, 2 if s % 6 == 5 else 1)
                if s in AHEAD:
                    split_unit(MIX0 + AHEAD.index(s), (MIX0 + AHEAD.index(s)) % RING)
                if s >= 2 * TT + 4 and (s - 4) % (2 * TT) == 0:
                    o_lo((s - 4) // (2 * TT) - 1)
            conv(done, CC * TAPS)

            def merge(m):
                n = MIX0 + MIX.index(("out", m))
                dve.wait_ge(w_used, n + 1)
                dve.wait_ge(sig_ok, CC + 2 * m + 2)
                a = mark(nc.vector.tensor_tensor(gate[:, 2 * (m % 2), :], gate[:, 2 * (m % 2), :], UB[n % 4][:, :], ALU.mult))
                b = mark(nc.vector.tensor_tensor(gate[:, 2 * (m % 2) + 1, :], gate[:, 2 * (m % 2) + 1, :], XB[m % 2][:, :],
                                                 ALU.mult))
                dve.wait_ge(step, b)
                nc.vector.tensor_tensor(wide[:, m, :], gate[:, 2 * (m % 2), :], gate[:, 2 * (m % 2) + 1, :],
                                        ALU.add).then_inc(m_ok, 1)

            dve.wait_ge(tap_ok, CC * TAPS)
            nc.vector.memset(small[:, 60:61], 0.0).then_inc(conv_ok, 1)
            o_lo(3)
            dve.wait_ge(y_sum, 1)
            link(nc.vector.tensor_scalar(rstd, XB[0][:, :], 1.0 / 512, None, ALU.mult))
            for i in range(CC):
                nc.vector.tensor_tensor(y[:, i, :], y[:, i, :], rstd, ALU.subtract).then_inc(y_ok, 1)
            split_unit(MIX0 + 3, (MIX0 + 3) % RING)
            dve.wait_ge(sq_used, 2 * DC + CC)
            norm_scale(512)
            split_unit(MIX0 + 4, (MIX0 + 4) % RING)
            for i in range(CC):
                nc.vector.tensor_tensor(y[:, i, :], y[:, i, :], rstd, ALU.mult).then_inc(y_nrm, 1)
            for i in range(CC):
                lo_part(mix_lo[:, i, :], y[:, i, :], mix_hi[:, i, :])
            for n in range(3):
                ada_rest(ADA_FIRST + n)
            for n in range(MIX0 + 3, WOUT0):
                split_unit(n + 2, (n + 2) % RING)
                ada_rest(ADA_FIRST + n - MIX0)
                if MIX[n - 1 - MIX0][0] == "out":
                    merge(MIX[n - 1 - MIX0][1])
            for m in range(DC - 1):
                lo_part(act_lo[:, m, :], wide[:, m, :], act_hi[:, m, :])
            merge(DC - 1)
            lo_part(act_lo[:, DC - 1, :], wide[:, DC - 1, :], act_hi[:, DC - 1, :])

            n1 = ADA_FIRST + WOUT0 - MIX0
            dve.wait_ge(ada_used, n1)
            link(nc.vector.tensor_tensor(mod[:, ADA_FIRST:n1], mod[:, ADA_FIRST:n1],
                                         col("b_ada", ADA_FIRST, n1 - ADA_FIRST), ALU.add))
            link(nc.vector.tensor_scalar(small[:, 16:24], mod[:, 4 * DC:5 * DC], 1.0, None, ALU.add))
            link(nc.vector.tensor_tensor(small[:, 16:24], small[:, 16:24], col("g2", 0, DC), ALU.mult))
            for n in range(WOUT0, WQ0 + 1):
                if n < WQ0:
                    split_unit(n + 2, (n + 2) % RING)
                    ada_rest(ADA_FIRST + n - MIX0)
                m = n - 1 - WOUT0
                if m >= 0:
                    dve.wait_ge(w_used, n)
                    nc.vector.scalar_tensor_tensor(out=x[:, m, :], in0=UB[(n - 1) % 4][:, :],
                                                   scalar=mod[:, 2 * DC + m:2 * DC + m + 1], in1=x[:, m, :],
                                                   op0=ALU.mult, op1=ALU.add).then_inc(x2_ok, 1)
                if m >= 2:
                    add_squares(m - 1, 1)
            dve.wait_ge(ada_used, ADA)
            link(nc.vector.tensor_tensor(mod[:, n1:ADA], mod[:, n1:ADA], col("b_ada", n1, ADA - n1), ALU.add))
            dve.wait_ge(step, count["step"])
            dve.wait_ge(sq_used, 3 * DC + CC)
            normalised(False, lambda m: None)

            def topk(tt, h):
                if h == 0 and tt == 0:
                    dve.wait_ge(a_lo, lo)
                dve.wait_ge(sc_ok, 2 * h + 2)
                last = {}
                for part in range(5):
                    for p in range(2):
                        s = scores[:, tt, 2 * h + p, :]
                        v, ix = sv[:, tt, 2 * h + p, :], si[:, tt, 2 * h + p, :]
                        if part:
                            dve.wait_ge(step, last[p])
                        if part == 0:
                            ins = nc.vector.max(v[:, 0:8], s)
                        elif part == 1:
                            ins = nc.vector.max_index(ix[:, 0:8], v[:, 0:8], s)
                        elif part == 2:
                            ins = nc.vector.match_replace(mr[:, p, :], v[:, 0:8], s, LOWEST)
                        elif part == 3:
                            ins = nc.vector.max(v[:, 8:16], mr[:, p, :])
                        else:
                            ins = nc.vector.max_index(ix[:, 8:16], v[:, 8:16], mr[:, p, :])
                        last[p] = mark(ins)
                a = sv[:, tt, 2 * h, :].rearrange("p (k o) -> p k o", o=1).to_broadcast([P, TOPK, TOPK])
                b = sv[:, tt, 2 * h + 1, :].rearrange("p (o k) -> p o k", o=1).to_broadcast([P, TOPK, TOPK])
                link(nc.vector.tensor_tensor(cand.rearrange("p (a b) -> p a b", b=TOPK), a, b, ALU.add))
                link(nc.vector.max(top[:, tt, h, 0:8], cand))
                mark(nc.vector.max_index(pos[:, tt, h, 0:8], top[:, tt, h, 0:8], cand))
                link(nc.vector.match_replace(cand2, top[:, tt, h, 0:8], cand, LOWEST))
                link(nc.vector.max(top[:, tt, h, 8:16], cand2))
                link(nc.vector.max_index(pos[:, tt, h, 8:16], top[:, tt, h, 8:16], cand2))

            for h in range(PH):
                for tt in range(TT):
                    topk(tt, h)
            link(nc.vector.tensor_copy(small[:, 80:112].rearrange("p (t h) -> p t h", t=TT), top[:, :, :, 0]))
            for tt in range(TT):
                nc.vector.tensor_tensor(top[:, tt, :, :], top[:, tt, :, :],
                                        small[:, 80 + PH * tt:80 + PH * tt + PH].rearrange(
                                            "p (h o) -> p h o", o=1).to_broadcast([P, PH, TOPK]), ALU.subtract
                                        ).then_inc(tk_ok, 1)
            eq = hot16.rearrange("p (c r) -> p c r", r=TOPK)
            eq4 = hot16.rearrange("p (h k r) -> p h k r", h=PH, k=TOPK)
            def indices(at_, tt, part):
                pv = pos[:, tt, :, :].rearrange("p h k -> p (h k)")
                if part == 0:
                    mark(nc.vector.tensor_scalar(ranku[:, 0, :], pv, 4, None, ALU.logical_shift_right))
                    mark(nc.vector.tensor_scalar(ranku[:, 1, :], pv, 15, None, ALU.bitwise_and))
                    link(nc.vector.tensor_copy(sif, si[:, tt, :, :].rearrange("p c k -> p (c k)")))
                    link(nc.vector.tensor_copy(rank[:, :, :], ranku[:, :, :]))
                    if at_ >= 2:
                        dve.wait_ge(ijt_ok, at_ - 1)
                if part < 2:
                    link(nc.vector.tensor_tensor(eq, rank[:, part, :].rearrange("p (c o) -> p c o", o=1).to_broadcast(
                        [P, P, TOPK]), iota16.rearrange("p (o r) -> p o r", o=1).to_broadcast([P, P, TOPK]),
                        ALU.is_equal))
                    six = sif.rearrange("p (h two r) -> p h two r", h=PH, two=2)[:, :, part:part + 1, :]
                    link(nc.vector.tensor_tensor(eq4, eq4, six.to_broadcast([P, PH, TOPK, TOPK]), ALU.mult))
                    link(nc.vector.tensor_reduce(ijw[:, part, :], eq, AX.X, ALU.add))
                if part == 2:
                    dve.wait_ge(te_ok, TT)
                    e = top[:, tt, :, :]
                    link(nc.vector.tensor_reduce(small[:, 64:72], e, AX.X, ALU.add))
                    link(nc.vector.reciprocal(small[:, 72:80], small[:, 64:72]))
                    nc.vector.tensor_tensor(ijw[:, 2, :].rearrange("p (h k) -> p h k", h=PH), e,
                                            small[:, 72:80].rearrange("p (h o) -> p h o", o=1).to_broadcast(
                                                [P, PH, TOPK]), ALU.mult).then_inc(ijw_ok, 1)
                    dve.wait_ge(ijw_ok, at_ + 1)
                    if tt == GT:
                        mark(nc.vector.scalar_tensor_tensor(out=idx3[:, 0, :], in0=ijw[:, 0, :], scalar=float(NKEY),
                                                            in1=ijw[:, 1, :], op0=ALU.mult, op1=ALU.add))
                        mark(nc.vector.scalar_tensor_tensor(out=idx3[:, 1, :], in0=ijw[:, 1, :], scalar=float(NKEY),
                                                            in1=ijw[:, 0, :], op0=ALU.mult, op1=ALU.add))
                        link(nc.vector.tensor_copy(w3, ijw[:, 2, :]))
                        nc.vector.memset(small[:, 61:62], 0.0).then_inc(idx_ok, 1)

            def dot(k4, b):
                dve.wait_ge(row_in[b], (k4 + 1) * 16)
                nc.vector.tensor_tensor_reduce(rows[:, b, :], rows[:, b, :], htok[:, :], 1.0, 0.0, ALU.mult, ALU.add,
                                               dot4[:, b:b + 1]).then_inc(dot_ok, 1)
                if b == 3:
                    dve.wait_ge(dot_ok, k4 * 4 + 4)
                    nc.vector.tensor_copy(dots[:, bass.ds(k4 * 4, 4)], dot4).then_inc(d4_ok, 1)
                    dve.wait_ge(d4_ok, k4 + 1)

            for at_ in range(TT):
                for part in range(3):
                    indices(at_, (GT + at_) % TT, part)
                if at_ == 1:
                    dve.wait_ge(ht_cp, 2)
                for k4 in {1: (0,), 2: (1,), 3: (2, 3)}.get(at_, ()):
                    for b in range(4):
                        dot(k4, b)

            dve.wait_ge(ijt_cp, 3 * DT)

            dve.wait_ge(w_split, POOL_LAST)

            def g_turn(it, first):
                for b in range(G_UNITS):
                    split_unit(it * G_UNITS + (FRONT + G_FIRST + b + 2), (b + 2) % RING)
                    for t in range(8 * b, 8 * b + 8):
                        if t % 4 == 0 and not (first and t < 8):
                            dve.wait_ge(g_ok, it * (2 * TB // 4) + (t // 4 - 1))
                        icol, jcol, wcol = (ijt[:, c, bass.ds(it * (2 * TB) + t, 1)] for c in range(3))
                        nc.vector.tensor_scalar(hot[:, t % 8, 0, :], iota, icol, None, ALU.is_equal).then_inc(hot_ok, 1)
                        if t % 8 not in ACT_HOTS:
                            nc.vector.tensor_scalar(hot[:, t % 8, 1, :], niota, jcol, wcol, ALU.is_equal, ALU.mult
                                                    ).then_inc(hot_ok, 1)
                        if t % 16 in (3, 7, 11):
                            d = t // 16 * 3 + t % 16 // 4
                            dot(it * (G_DOTS // 4) + (EARLY_DOTS // 4 + d // 4), d % 4)

            g_turn(0, True)
            with dve.Fori(1, G_TURNS) as it:
                g_turn(it, False)

            for b in range(4):
                split_unit(FRONT + G_LAST + b + 2, (b + 2) % RING)
                for d in (2 * b, 2 * b + 1):
                    dot(DOTS_A // 4 + d // 4, d % 4)
            with dve.Fori(1, LATE_TURNS) as turn:
                for b in range(4):
                    split_unit(turn * 4 + (FRONT + G_LAST + b + 2), (b + 2) % RING)
                    dot(turn + (DOTS_A // 4 + 1), b)

            def multiply(r, t, b):
                s = b // 4 % 2
                if b % 4 == 0:
                    dve.wait_ge(gt_in[s], (t + (b // 8 + 1)) * 16)
                    dve.wait_ge(at_in[s], (t + (b // 8 + 1)) * 16)
                if not isinstance(r, int) or r >= 2:
                    dve.wait_ge(c_lo, r - 1)
                nc.vector.tensor_tensor(cf[:, b % 2, :].rearrange("p (b t) -> p b t", t=TB),
                                        atile[:, s, b % 4, :].rearrange("p (b t) -> p b t", t=TB),
                                        gtile[:, s, :, b % 4, :], ALU.mult).then_inc(c_mul, 1)

            def coef_lo(r, b):
                dve.wait_ge(c_hi, r + 1)
                nc.vector.tensor_tensor(mix_lo[:, b % C_RING, 0:ND], cf[:, b % 2, :],
                                        mix_hi[:, b % C_RING, 0:ND].bitcast(F32), ALU.subtract).then_inc(c_lo, 1)

            for b in range(4):
                if b:
                    multiply(b - 1, 0, b - 1)
                split_unit(VBASE - 4 + b + 2, (b + 2) % RING)
                if b:
                    coef_lo(b - 1, b - 1)
            nc.vector.memset(acc, 0.0).then_inc(acc_ok, 1)
            dve.wait_ge(g3_ok, 1)
            link(nc.vector.tensor_tensor(w3, w3, g3, ALU.mult))

            def v_turn(t, last):
                for b in range(C_RING):
                    r = t * C_RING + b
                    more = not (last and b + C_LEAD >= C_RING)
                    if more:
                        multiply(r + C_LEAD, t, b + C_LEAD)
                    if not (last and b + 2 >= C_RING):
                        split_unit(r + (VBASE + 2), (b + 2) % RING)
                    if more:
                        coef_lo(r + C_LEAD, b + C_LEAD)
                    dve.wait_ge(row_in[b % 4], (t * 2 + (PICKS // 4 + b // 4 + 1)) * 16)
                    dve.wait_ge(acc_ok, r + 1)
                    nc.vector.scalar_tensor_tensor(out=acc, in0=rows[:, b % 4, :], scalar=w3[:, bass.ds(r, 1)],
                                                   in1=acc, op0=ALU.mult, op1=ALU.add).then_inc(acc_ok, 1)

            v_turn(0, False)
            with dve.Fori(1, SLABS // C_RING - 1) as t:
                v_turn(t, False)
            v_turn(SLABS // C_RING - 1, True)

            dve.wait_ge(x2_in, 16)
            for m in range(DC):
                dve.wait_ge(t3_ok, m + 1)
                nc.vector.scalar_tensor_tensor(out=wide[:, m, :], in0=bank[m][:, :],
                                               scalar=mod[:, 5 * DC + m:5 * DC + m + 1], in1=wide[:, m, :],
                                               op0=ALU.mult, op1=ALU.add).then_inc(fin_ok, 1)

        @block.tensor
        def _(pe):
            sums = 0

            def sum_squares(m, n, lhs=None, out=None):
                nonlocal sums
                pe.wait_ge(sq_ok, sums + 1)
                nc.tensor.matmul(STAT[:, :] if out is None else out, ones if lhs is None else lhs,
                                 sq[:, sums % 2, :], start=(m == 0), stop=(m == n - 1)).then_inc(sq_used, 1)
                sums += 1

            def product(out, slot, dcs, rhs_hi, rhs_lo, col0=0):
                for i, dc in enumerate(dcs):
                    w = slice(col0 + dc * P, col0 + (dc + 1) * P)
                    nc.tensor.matmul(out, w_hi[:, slot, w], rhs_hi[:, dc, :], start=(i == 0), stop=False)
                    nc.tensor.matmul(out, w_hi[:, slot, w], rhs_lo[:, dc, :], start=False, stop=False)
                    last = nc.tensor.matmul(out, w_lo[:, slot, w], rhs_hi[:, dc, :], start=False,
                                            stop=(i == len(dcs) - 1))
                return last

            def unit(n):
                pe.wait_ge(w_split, n + 1)
                if n >= 4:
                    pe.wait_ge(*sums_read(n - 4))
                product(UB[n % 4][:, :], n % RING, range(DC), act_hi, act_lo).then_inc(w_used, 1)

            def pair_chunk(n, dc, first_lo):
                pe.wait_ge(a_lo, first_lo + dc + 1)
                w = slice(dc * P, (dc + 1) * P)
                for j in (n, n + 1):
                    if dc == 0:
                        pe.wait_ge(w_split, j + 1)
                        if j >= 4:
                            pe.wait_ge(*sums_read(j - 4))
                    out = UB[j % 4][:, :]
                    nc.tensor.matmul(out, w_hi[:, j % RING, w], act_hi[:, dc, :], start=(dc == 0), stop=False)
                    nc.tensor.matmul(out, w_hi[:, j % RING, w], act_lo[:, dc, :], start=False, stop=False)
                    last = nc.tensor.matmul(out, w_lo[:, j % RING, w], act_hi[:, dc, :], start=False, stop=(dc == DC - 1))
                    if dc == DC - 1:
                        last.then_inc(w_used, 1)

            def norm_sums(k):
                nonlocal sums
                pe.wait_ge(sa_ok, (k + 1) * (DC - 2))
                nc.tensor.matmul(STAT[:, :], ones, sqsum[k], start=True, stop=False)
                sums += DC
                pe.wait_ge(sq_ok, sums)
                nc.tensor.matmul(STAT[:, :], ones, sq[:, 1, :], start=False, stop=True).then_inc(sq_used, DC)

            pe.wait_ge(ones_ok, 1)
            norm_sums(0)
            for dc in range(DC):
                pair_chunk(0, dc, 0)
            for n in range(2, V0):
                unit(n)
                if n > QK0:
                    sum_squares(n - 1 - QK0, DC, sel[:, n - 1 - QK0, :], STAT[0:16, :])
            sum_squares(DC - 1, DC, sel[:, DC - 1, :], STAT[0:16, :])
            pe.wait_ge(selt_in, 16)
            pe.wait_ge(par_in, 32)
            pe.wait_ge(w_split, MIX0)
            def spread(m):
                if m == 0:
                    pe.wait_ge(ms_ok, 3)
                if m >= 2:
                    pe.wait_ge(qkn_ok, m - 1)
                nc.tensor.matmul(XB[m % 2][:, :], selt[:, m * P:(m + 1) * P], rstd[0:16, :],
                                 start=True, stop=True).then_inc(rb_ok, 1)

            spreads = 0
            for tt in range(TT):
                pe.wait_ge(*sums_read(V0 - 4 + tt))
                t = slice(tt * P, (tt + 1) * P)
                for dc in range(DC):
                    w = slice(dc * P, (dc + 1) * P)
                    nc.tensor.matmul(UB[tt][:, :], act_hi[:, dc, t], w_hi[:, :, w], start=(dc == 0), stop=False)
                    nc.tensor.matmul(UB[tt][:, :], act_hi[:, dc, t], w_lo[:, :, w], start=False, stop=False)
                    last = nc.tensor.matmul(UB[tt][:, :], act_lo[:, dc, t], w_hi[:, :, w], start=False,
                                            stop=(dc == DC - 1))
                    if tt >= 1 and dc % 3 == 1 and spreads < DC:
                        spread(spreads)
                        spreads += 1
                if tt < TT - 1:
                    last.then_inc(v_sum, 1)
                else:
                    last.then_inc(w_used, RING)

            for s in range(HEADS * TT + LAG + 1):
                if s < HEADS * TT:
                    h, q = divmod(s, TT)
                    base = HD * (h % 2)
                    n = (q + 1) * P
                    if h % 2 == 0 and q == 0:
                        pe.wait_ge(qkn_ok, DC // 2 + h // 2 + 1)
                    if s == 2:
                        pe.wait_ge(qkn_ok, DC)
                    if s >= 4:
                        pe.wait_ge(sb_ok, s - 3)
                    nc.tensor.matmul(SB[s % 4][:, 0:n], wide[base:base + HD, h // 2, q * P:(q + 1) * P],
                                     wide[base:base + HD, 4 + h // 2, 0:n], start=True, stop=True).then_inc(s_ok, 1)
                r = s - LAG
                if 0 <= r < HEADS * TT:
                    pe.wait_ge(p_ok, r + 1)
                    if r == 0:
                        pe.wait_ge(v_ok, TT)
                    if r >= 2:
                        pe.wait_ge(pt_ok, r - 1)
                    for b in range(r % TT + 1):
                        last = nc.tensor.transpose(UB[r % 2][:, b * P:(b + 1) * P], sc[:, r % SC, b * P:(b + 1) * P], ident)
                    last.then_inc(t_ok, 1)
                r = s - LAG - 1
                if r >= 0 and r % TT == TT - 1:
                    h = r // TT
                    pair = h // 2
                    if pair >= 2 and h % 2 == 0:
                        pe.wait_ge(a_lo, DC + pair - 1)
                    pe.wait_ge(pt_ok, r + 1)
                    base = HD * (h % 2)
                    for kb in range(TT):
                        last = nc.tensor.matmul(UB[2 + pair % 2][base:base + HD, kb * P:T],
                                                vtok[:, kb, h * HD:(h + 1) * HD], pt[:, h % 2, kb, kb * P:T],
                                                start=(kb == 0), stop=(kb == TT - 1))
                    last.then_inc(o_ok, 1)

            pe.wait_ge(pt_ok, HEADS * TT)
            pe.wait_ge(sb_ok, HEADS * TT)

            def mix_unit(n):
                kind = MIX[n - MIX0]
                if kind[0] == "gate":
                    if n - MIX0 < 4 and n % 4 >= 2:
                        pe.wait_ge(a_lo, DC + CC)
                    unit(n)
                    return
                m = kind[1]
                pe.wait_ge(w_split, n + 1)
                pe.wait_ge(*sums_read(n - 4))
                if m >= 2:
                    pe.wait_ge(m_ok, m - 1)
                if m == 0:
                    pe.wait_ge(a_lo, DC + 2 * CC)
                product(UB[n % 4][:, :], n % RING, range(CC), mix_hi, mix_lo)
                product(XB[m % 2][:, :], n % RING, range(CC, 2 * CC), mix_hi, mix_lo).then_inc(w_used, 1)

            pe.wait_ge(conv_ok, 1)
            for i in range(CC):
                last = nc.tensor.matmul(XB[0][:, :], ones, y[:, i, :], start=(i == 0), stop=(i == CC - 1))
            last.then_inc(y_sum, 1)
            mix_unit(MIX0)
            for i in range(CC):
                sum_squares(i, CC)
            for n in range(MIX0 + 1, WOUT0):
                mix_unit(n)
            merged_lo = DC + 2 * CC
            for dc in range(DC):
                pair_chunk(WOUT0, dc, merged_lo)
            for n in range(WOUT0 + 2, WQ0):
                unit(n)
            norm_sums(1)

            h2_lo = merged_lo + DC

            def key_scores(c):
                pe.wait_ge(qf_ok, c + 1)
                if c == 0:
                    pe.wait_ge(ht_cp, 2)
                if c >= 2:
                    pe.wait_ge(sc_ok, c - 1)
                for tt in range(TT):
                    last = nc.tensor.matmul(XB[c % 2][:, tt * P:(tt + 1) * P], qf[:, c % 2, tt * P:(tt + 1) * P],
                                            keys[:, c, :], start=True, stop=True)
                last.then_inc(ks_ok, 1)

            for m in range(DC + 2):
                if m < DC:
                    pe.wait_ge(a_pre, DC + m + 1)
                    nc.tensor.transpose(XB[m // 4][:, m % 4 * P:(m % 4 + 1) * P], nrm[:, NS[m % 4], GT * P:(GT + 1) * P],
                                        ident).then_inc(ht_ok, 1)
                if m >= 2:
                    pair_chunk(WQ0, m - 2, h2_lo)
            pe.wait_ge(keys_in, 16)
            key_scores(0)
            for c in range(2, 2 * PH):
                unit(WQ0 + c)
                key_scores(c - 1)
            key_scores(2 * PH - 1)
            pe.wait_ge(sc_ok, 2 * PH)

            def slab(t, per, b):
                q = t * per + b
                pe.wait_ge(w_split, q + (FRONT + 1))
                if isinstance(q, int) and q < 4:
                    pe.wait_ge(*sums_read(FRONT - 4 + q))
                else:
                    pe.wait_ge(ge_ok, q - 3)
                product(UB[b % 4][:, 0:ND], b % RING, range(DC), act_hi[:, :, 0:ND], act_lo[:, :, 0:ND]
                        ).then_inc(w_used, 1)

            for q in range(4):
                slab(0, 4, q)
            with pe.Fori(1, EARLY_SLAB // 4) as turn:
                for b in range(4):
                    slab(turn, 4, b)
            for q in range(EARLY_SLAB, G_FIRST):
                slab(0, 4, q)
                if q in LIST_SLABS:
                    tt = LIST_SLABS.index(q)
                    pe.wait_ge(ijw_ok, tt + 2)
                    if tt >= 2:
                        pe.wait_ge(ijt_cp, 3 * (tt - 1))
                    for c in range(3):
                        last = nc.tensor.transpose(XB[tt % 2][:, c * P:(c + 1) * P], ijw[:, c, :], ident)
                    last.then_inc(ijt_ok, 1)
            pe.wait_ge(ijt_cp, 3 * DT)

            def g_turn(it, first):
                for b in range(G_UNITS):
                    slab(it, G_UNITS, G_FIRST + b)
                    for t in range(8 * b, 8 * b + 8):
                        j = t // 4
                        if t % 4 == 0 and not (first and j < 4):
                            pe.wait_ge(g_cp, it * (2 * TB // 4) + (j - 3))
                        on_act = sum(x % 8 in ACT_HOTS for x in range(t + 1))
                        if t % 8 in ACT_HOTS:
                            pe.wait_ge(hotw_ok, it * (len(ACT_HOTS) * G_UNITS) + on_act)
                        pe.wait_ge(hot_ok, it * ((16 - len(ACT_HOTS)) * G_UNITS) + (2 * (t + 1) - on_act))
                        last = nc.tensor.matmul(bank[j % 4][:, (t % 4) * P:(t % 4 + 1) * P], hot[:, t % 8, 0, :],
                                                hot[:, t % 8, 1, :], start=True, stop=True)
                        if t % 4 == 3:
                            last.then_inc(g_ok, 1)

            g_turn(0, True)
            with pe.Fori(1, G_TURNS) as it:
                g_turn(it, False)
            with pe.Fori(G_LAST // 4, SLABS // 4) as turn:
                for b in range(4):
                    slab(turn, 4, b)

            pe.wait_ge(g_cp, ND // 4)

            def v_slab(r, b, first=False, final=False):
                pe.wait_ge(w_split, r + (VBASE + 1))
                pe.wait_ge(c_lo, r + 1)
                for m in range(DC):
                    if first and m >= 4:
                        pe.wait_ge(ge_ok, SLABS - 7 + m)
                    w = slice(m * P, (m + 1) * P)
                    slot, c = b % RING, b % C_RING
                    nc.tensor.matmul(bank[m][:, 0:ND], w_hi[:, slot, w], mix_hi[:, c, 0:ND], start=first, stop=False)
                    nc.tensor.matmul(bank[m][:, 0:ND], w_hi[:, slot, w], mix_lo[:, c, 0:ND], start=False, stop=False)
                    last = nc.tensor.matmul(bank[m][:, 0:ND], w_lo[:, slot, w], mix_hi[:, c, 0:ND], start=False, stop=final)
                last.then_inc(w_used, 1)

            for b in range(C_RING):
                v_slab(b, b, first=(b == 0))
            with pe.Fori(1, SLABS // C_RING - 1) as t:
                for b in range(C_RING):
                    v_slab(t * C_RING + b, b)
            for b in range(C_RING):
                v_slab(SLABS - C_RING + b, b, final=(b == C_RING - 1))
            pe.wait_ge(acc_ok, PICKS + 1)
            for m in range(DC):
                nc.tensor.transpose(bank[m][:, ND:T], acc[:, m * P:(m + 1) * P], ident).then_inc(t3_ok, 1)


def layouts(i):
    f = lambda a: np.ascontiguousarray(np.asarray(a))

    def units(w):
        k, n = w.shape
        return w.reshape(k // P, P, n // P, P).transpose(2, 1, 0, 3).reshape(n // P, P, k)

    def cols(v):
        return np.asarray(v).reshape(-1, P).T

    w = {k: np.asarray(v) for k, v in i.items()}
    w_in = units(w["w_in"][0])
    w_mix = np.concatenate([units(w["w_conv_out"][0]), units(w["w_attn_out"][0])], axis=2)
    order = []
    for b in range(CC):
        order += [w_in[CC + b], w_in[b]]
    order += [w_in[8 + m] for m in range(12)]
    for kind in MIX:
        order.append(w_in[20 + DC * kind[2] + kind[1]] if kind[0] == "gate" else w_mix[kind[1]])
    order += list(units(w["w_out"][0])) + list(units(w["peer_wq"][0]))
    w_ada = w["w_ada"][0].T.reshape(ADA, P, D)
    w_ada = np.concatenate([w_ada[:ADA_FIRST].reshape(2, DC, P, D)[::-1].transpose(1, 0, 2, 3).reshape(ADA_FIRST, P, D),
                            w_ada[ADA_FIRST:]])
    dw = w["conv_dw"][0].reshape(TAPS, CC, P).transpose(2, 1, 0).reshape(P, CC * TAPS)
    par = np.concatenate([cols(w["b_ada"][0]), cols(w["norm1_g"][0]), cols(w["norm2_g"][0]), dw,
                          cols(w["conv_b"][0]), cols(w["conv_ln_g"][0]), cols(w["conv_ln_b"][0]),
                          np.tile(w["q_norm_g"][0], 2)[:, None], np.tile(w["k_norm_g"][0], 2)[:, None]], axis=1)
    const = np.zeros((P, 5 * P), np.float32)
    const[:, 0:P] = np.eye(P)
    const[:, P:2 * P] = np.arange(P)
    for m in range(8):
        const[0:64, 2 * P + 16 * m + 2 * m] = 1.0
        const[64:128, 2 * P + 16 * m + 2 * m + 1] = 1.0
    const[:, 3 * P:3 * P + 16] = np.arange(16)
    const[:, 4 * P:5 * P] = -np.arange(P)
    selt = np.zeros((16, 8 * P), np.float32)
    for m in range(8):
        selt[2 * m, m * P:m * P + 64] = 1.0
        selt[2 * m + 1, m * P + 64:(m + 1) * P] = 1.0
    rel = np.clip(np.arange(P)[:, None] - np.arange(T)[None, :] + 384, -128, 128) + 128
    toep = w["rel_bias"][0][:, rel].transpose(1, 0, 2)
    keys = w["peer_keys"][0].reshape(2 * PH, NKEY, P).transpose(2, 0, 1)
    u = w["peer_u"][0].reshape(NKEY, NKEY, DC, P).transpose(1, 3, 2, 0).reshape(NKEY, P, D)
    v = w["peer_v"][0].reshape(NKEY, NKEY, D).transpose(1, 0, 2)
    return {
        "w_front": f(np.stack(order)), "w_ada": f(w_ada), "c": f(w["c"]), "par": f(par), "const": const,
        "selt": selt, "x": f(w["x"][0].T.reshape(DC, P, T)), "toep": f(toep), "keys": f(keys), "u": f(u), "v": f(v),
        "u_rows": f(w["peer_u"][0]),
    }


def kernel(**inputs):
    import concourse.bacc as bacc
    from concourse.bass_utils import run_bass_kernel_spmd

    arrays = layouts(inputs)
    nc = bacc.Bacc("TRN2", target_bir_lowering=False, num_devices=1)
    aps = [nc.dram_tensor(f"{k}_dram", a.shape, F32, kind="ExternalInput").ap() for k, a in arrays.items()]
    g_d = nc.dram_tensor("g_scratch", (ND // TB, P, NKEY * TB), F32, kind="Internal").ap()
    a_d = nc.dram_tensor("a_scratch", (SLABS, P, ND), F32, kind="Internal").ap()
    x2_d = nc.dram_tensor("x2_scratch", (DC, P, T), F32, kind="Internal").ap()
    out_d = nc.dram_tensor("out_dram", (DC, P, T), F32, kind="ExternalOutput").ap()
    block_program(nc, *aps, g_d, a_d, x2_d, out_d)
    r = run_bass_kernel_spmd(nc, [{f"{k}_dram": a for k, a in arrays.items()}], core_ids=[0])
    return np.ascontiguousarray(r.results[0]["out_dram"].reshape(1, D, T).transpose(0, 2, 1))
```
